# Optimizing a Trainium2 kernel written in Bass

```python
import math
import jax, jax.numpy as jnp
from jax import lax
import numpy as np

D_MODEL = 1024
BATCH = 1
SEQ = 512
DEPTH = 2
DEC_BATCH = 8
DEC_SEQ = 8
PAST_LEN = 256
PAGE_SIZE = 128

N_MIXERS = 2
N_A_LAYERS = (DEPTH + 1) // 2
N_B_LAYERS = DEPTH // 2

A_HEADS = 8
A_KDIM = 128
A_VDIM = 256
A_QK_WIDTH = A_HEADS * A_KDIM
A_V_WIDTH = A_HEADS * A_VDIM
A_CHUNK = 32

B_GROUPS = ((128, 1), (512, 4), (2048, 16))
B_HEADS_PER_GROUP = 4
B_HEAD_DIM = 128
B_N_HEADS = len(B_GROUPS) * B_HEADS_PER_GROUP
B_WIDTH = B_N_HEADS * B_HEAD_DIM
B_QBLOCK = 128
ROPE_THETA = 10000.0
EPS = 1e-6

kernel_name = 'hgrn2_dilated_swa_adaln_decode_step'

def rmsnorm(x, w):
    xf = x.astype(jnp.float32)
    y = xf * lax.rsqrt(jnp.mean(xf * xf, axis=-1, keepdims=True) + EPS)
    return (y * w.astype(jnp.float32)).astype(x.dtype)

def adaln(x, c, norm_w, w_ada, b_ada):
    ada = jax.nn.silu(c) @ w_ada + b_ada
    shift, scale, gate = jnp.split(ada, 3, axis=-1)
    h = rmsnorm(x, norm_w) * (1 + scale[:, None]) + shift[:, None]
    return h, gate[:, None]

def rope(x, pos):
    half = x.shape[-1] // 2
    inv = ROPE_THETA ** (-jnp.arange(half, dtype=jnp.float32) / half)
    ang = pos.astype(jnp.float32)[:, None] * inv[None]
    cos = jnp.cos(ang)[None, :, None, :]
    sin = jnp.sin(ang)[None, :, None, :]
    xf = x.astype(jnp.float32)
    x1, x2 = xf[..., :half], xf[..., half:]
    return jnp.concatenate([x1 * cos - x2 * sin, x2 * cos + x1 * sin], axis=-1).astype(x.dtype)

def hgrn2_scan(q, k, v, logf, s0):
    B, L, H, dk = q.shape
    dv = v.shape[-1]
    C = math.gcd(L, A_CHUNK)
    n = L // C

    def to_chunks(a):
        return a.reshape(B, n, C, H, a.shape[-1]).transpose(1, 0, 3, 2, 4)

    causal = jnp.tril(jnp.ones((C, C), dtype=bool))

    def step(S, inp):
        qc, kc, vc, gc = inp
        b = jnp.cumsum(gc, axis=2)
        rel = jnp.where(causal[None, None, :, :, None],
                        b[:, :, :, None, :] - b[:, :, None, :, :], -jnp.inf)
        A = jnp.einsum('bhtc,bhsc,bhtsc->bhts', qc, kc, jnp.exp(rel))
        o = (jnp.einsum('bhts,bhsv->bhtv', A, vc)
             + jnp.einsum('bhtc,bhcv->bhtv', qc * jnp.exp(b), S))
        b_last = b[:, :, -1:, :]
        S_new = (jnp.exp(b_last[:, :, 0, :])[..., None] * S
                 + jnp.einsum('bhsc,bhsv->bhcv', kc * jnp.exp(b_last - b), vc))
        return S_new, o

    S, o = lax.scan(step, s0, (to_chunks(q), to_chunks(k), to_chunks(v), to_chunks(logf)))
    o = o.transpose(1, 0, 3, 2, 4).reshape(B, L, H, dv)
    return o, S

def hgrn2_mixer(h, s0, lb, w_in, b_f, g_norm_w, w_out):
    B, L, _ = h.shape
    proj = h @ w_in
    q, f, i, z = jnp.split(proj, [A_QK_WIDTH, 2 * A_QK_WIDTH, 2 * A_QK_WIDTH + A_V_WIDTH], axis=-1)
    q = jax.nn.silu(q.astype(jnp.float32)).reshape(B, L, A_HEADS, A_KDIM)
    f = lb + (1.0 - lb) * jax.nn.sigmoid((f + b_f).astype(jnp.float32))
    logf = jnp.log(f).reshape(B, L, A_HEADS, A_KDIM)
    k = (1.0 - f).reshape(B, L, A_HEADS, A_KDIM)
    v = i.astype(jnp.float32).reshape(B, L, A_HEADS, A_VDIM)
    o, S = hgrn2_scan(q, k, v, logf, s0.astype(jnp.float32))
    o = rmsnorm(o, g_norm_w).reshape(B, L, A_V_WIDTH).astype(h.dtype)
    y = (o * jax.nn.silu(z)) @ w_out
    return y, S.astype(s0.dtype)

def dilated_window_attn(q, k, v, q_start, k_start, dilation, n_keys):
    B, Lq, Hg, hd = q.shape
    QB = math.gcd(Lq, B_QBLOCK)
    nb = Lq // QB
    offs = jnp.arange(n_keys, dtype=jnp.int32) * dilation
    scale = hd ** -0.5

    def block(args):
        qb, bi = args
        qpos = q_start + bi * QB + jnp.arange(QB, dtype=jnp.int32)
        kidx = qpos[:, None] - offs[None, :] - k_start
        valid = kidx >= 0
        kidx = jnp.maximum(kidx, 0)
        kg = k[:, kidx].astype(jnp.float32)
        vg = v[:, kidx].astype(jnp.float32)
        s = jnp.einsum('bqhd,bqnhd->bqhn', qb.astype(jnp.float32), kg) * scale
        s = jnp.where(valid[None, :, None, :], s, -jnp.inf)
        lse = jax.nn.logsumexp(s, axis=-1)
        p = jnp.exp(s - lse[..., None])
        o = jnp.einsum('bqhn,bqnhd->bqhd', p, vg)
        return o, lse

    qblocks = q.reshape(B, nb, QB, Hg, hd).transpose(1, 0, 2, 3, 4)
    o, lse = lax.map(block, (qblocks, jnp.arange(nb, dtype=jnp.int32)))
    o = o.transpose(1, 0, 2, 3, 4).reshape(B, Lq, Hg, hd)
    lse = lse.transpose(1, 0, 2, 3).reshape(B, Lq, Hg)
    return o, lse

def dilated_mixer(h, pos, start, bufs, w_in, q_norm_w, k_norm_w, w_out):
    B, L, _ = h.shape
    proj = h @ w_in
    q, k, v, z = jnp.split(proj, 4, axis=-1)
    q = rope(rmsnorm(q.reshape(B, L, B_N_HEADS, B_HEAD_DIM), q_norm_w), pos)
    k = rope(rmsnorm(k.reshape(B, L, B_N_HEADS, B_HEAD_DIM), k_norm_w), pos)
    v = v.reshape(B, L, B_N_HEADS, B_HEAD_DIM)
    outs, lses, rows = [], [], []
    for g, (window, dil) in enumerate(B_GROUPS):
        sl = slice(g * B_HEADS_PER_GROUP, (g + 1) * B_HEADS_PER_GROUP)
        qg, kg, vg = q[:, :, sl], k[:, :, sl], v[:, :, sl]
        rows.append(jnp.stack([kg, vg], axis=2))
        if bufs is None:
            k_all, v_all, k_start = kg, vg, start
        else:
            buf = bufs[g]
            k_all = jnp.concatenate([buf[:, :, 0].astype(kg.dtype), kg], axis=1)
            v_all = jnp.concatenate([buf[:, :, 1].astype(vg.dtype), vg], axis=1)
            k_start = start - buf.shape[1]
        o, lse = dilated_window_attn(qg, k_all, v_all, start, k_start, dil, window // dil + 1)
        outs.append(o)
        lses.append(lse)
    lam = jax.nn.softmax(jnp.stack(lses, axis=0), axis=0)
    o = jnp.concatenate([outs[g] * lam[g][..., None] for g in range(len(B_GROUPS))], axis=2)
    o = o.reshape(B, L, B_WIDTH).astype(h.dtype)
    y = (o * jax.nn.silu(z)) @ w_out
    return y, rows

def trunk(x, c, start, state_hgrn, kv_bufs, norm_w, ada_w, ada_b, a_lower_bounds,
          a_w_in, a_b_f, a_g_norm_w, a_w_out, b_w_in, b_q_norm_w, b_k_norm_w, b_w_out):
    B, L, _ = x.shape
    pos = start + jnp.arange(L, dtype=jnp.int32)
    lb_all = jnp.cumsum(jax.nn.softmax(a_lower_bounds.astype(jnp.float32), axis=0), axis=0)
    new_hgrn = []
    new_kv = [[] for _ in B_GROUPS]
    for i in range(DEPTH):
        h, gate = adaln(x, c, norm_w[i], ada_w[i], ada_b[i])
        j = i // N_MIXERS
        if i % N_MIXERS == 0:
            if state_hgrn is None:
                s0 = jnp.zeros((B, A_HEADS, A_KDIM, A_VDIM), x.dtype)
            else:
                s0 = state_hgrn[j]
            y, s_new = hgrn2_mixer(h, s0, lb_all[i], a_w_in[j], a_b_f[j], a_g_norm_w[j], a_w_out[j])
            new_hgrn.append(s_new)
        else:
            bufs = None if kv_bufs is None else tuple(buf[j] for buf in kv_bufs)
            y, rows = dilated_mixer(h, pos, start, bufs, b_w_in[j], b_q_norm_w[j], b_k_norm_w[j], b_w_out[j])
            for g, (window, _) in enumerate(B_GROUPS):
                if kv_bufs is None:
                    new_kv[g].append(rows[g][:, L - min(window, L):])
                else:
                    new_kv[g].append(rows[g])
        x = x + gate * y
    kv_out = [jnp.stack(r, axis=0) for r in new_kv]
    return x, jnp.stack(new_hgrn, axis=0), kv_out[0], kv_out[1], kv_out[2]

def setup_inputs(seed: int = 0) -> dict:
    key = jax.random.key(seed)
    ks = jax.random.split(key, 24)
    nrm = jax.random.normal
    f32 = jnp.float32
    Hg, hd = B_HEADS_PER_GROUP, B_HEAD_DIM
    return {
        'x_prompt': nrm(ks[0], (BATCH, SEQ, D_MODEL), f32),
        'x_sample': nrm(ks[1], (DEC_BATCH, DEC_SEQ, D_MODEL), f32),
        'state_hgrn': 0.5 * nrm(ks[2], (N_A_LAYERS, DEC_BATCH, A_HEADS, A_KDIM, A_VDIM), f32),
        'cache_kv_w128': nrm(ks[3], (N_B_LAYERS, DEC_BATCH, min(128, PAST_LEN), 2, Hg, hd), f32),
        'cache_kv_w512': nrm(ks[4], (N_B_LAYERS, DEC_BATCH, min(512, PAST_LEN), 2, Hg, hd), f32),
        'cache_kv_w2048': nrm(ks[5], (N_B_LAYERS, DEC_BATCH, min(2048, PAST_LEN), 2, Hg, hd), f32),
        'c_prompt': nrm(ks[6], (BATCH, D_MODEL), f32),
        'c_sample': nrm(ks[7], (DEC_BATCH, D_MODEL), f32),
        'norm_w': 1.0 + 0.01 * nrm(ks[8], (DEPTH, D_MODEL), f32),
        'ada_w': 0.5 * D_MODEL ** -0.5 * nrm(ks[9], (DEPTH, D_MODEL, 3 * D_MODEL), f32),
        'ada_b': 0.01 * nrm(ks[10], (DEPTH, 3 * D_MODEL), f32),
        'a_lower_bounds': 0.1 * nrm(ks[11], (DEPTH, A_QK_WIDTH), f32),
        'a_w_in': D_MODEL ** -0.5 * nrm(ks[12], (N_A_LAYERS, D_MODEL, 2 * A_QK_WIDTH + 2 * A_V_WIDTH), f32),
        'a_b_f': 0.1 * nrm(ks[13], (N_A_LAYERS, A_QK_WIDTH), f32),
        'a_g_norm_w': 1.0 + 0.01 * nrm(ks[14], (N_A_LAYERS, A_VDIM), f32),
        'a_w_out': A_V_WIDTH ** -0.5 * nrm(ks[15], (N_A_LAYERS, A_V_WIDTH, D_MODEL), f32),
        'b_w_in': D_MODEL ** -0.5 * nrm(ks[16], (N_B_LAYERS, D_MODEL, 4 * B_WIDTH), f32),
        'b_q_norm_w': 1.0 + 0.01 * nrm(ks[17], (N_B_LAYERS, B_HEAD_DIM), f32),
        'b_k_norm_w': 1.0 + 0.01 * nrm(ks[18], (N_B_LAYERS, B_HEAD_DIM), f32),
        'b_w_out': B_WIDTH ** -0.5 * nrm(ks[19], (N_B_LAYERS, B_WIDTH, D_MODEL), f32),
    }

def reference(x_prompt, x_sample, state_hgrn, cache_kv_w128, cache_kv_w512, cache_kv_w2048,
              c_prompt, c_sample, norm_w, ada_w, ada_b, a_lower_bounds, a_w_in, a_b_f,
              a_g_norm_w, a_w_out, b_w_in, b_q_norm_w, b_k_norm_w, b_w_out):
    y_prompt, hgrn_prompt, kv128_prompt, kv512_prompt, kv2048_prompt = trunk(
        x_prompt, c_prompt, 0, None, None, norm_w, ada_w, ada_b, a_lower_bounds,
        a_w_in, a_b_f, a_g_norm_w, a_w_out, b_w_in, b_q_norm_w, b_k_norm_w, b_w_out)
    y_sample, hgrn_sample, kv128_sample, kv512_sample, kv2048_sample = trunk(
        x_sample, c_sample, PAST_LEN, state_hgrn, (cache_kv_w128, cache_kv_w512, cache_kv_w2048),
        norm_w, ada_w, ada_b, a_lower_bounds, a_w_in, a_b_f, a_g_norm_w, a_w_out,
        b_w_in, b_q_norm_w, b_k_norm_w, b_w_out)
    return (y_prompt, y_sample, hgrn_prompt, hgrn_sample, kv128_prompt, kv128_sample,
            kv512_prompt, kv512_sample, kv2048_prompt, kv2048_sample)


_drawn_inputs = setup_inputs


def setup_inputs(seed=0):
    import zlib

    import numpy as np

    out = dict(_drawn_inputs(seed))
    spreads = {}
    factors = {'cache_kv_w128': 5.913,
     'cache_kv_w512': 8.0,
     'cache_kv_w2048': 8.0,
     'norm_w': 5.781,
     'a_g_norm_w': 8.0,
     'b_q_norm_w': 8.0,
     'b_k_norm_w': 8.0,
     'a_b_f': 3.167}
    for name, (base, spread) in spreads.items():
        noise = np.random.default_rng([zlib.crc32(name.encode()), seed]).standard_normal(out[name].shape)
        drawn = base * np.exp(spread * noise) if base else spread * noise
        out[name] = __import__('jax').numpy.asarray(drawn.astype(out[name].dtype))
    for name, factor in factors.items():
        out[name] = (out[name] * factor).astype(out[name].dtype)
    return out
```

```python
from contextlib import ExitStack

import numpy as np

import concourse.bass as bass
from concourse import mybir

F32 = mybir.dt.float32
F32R = mybir.dt.float32r
U8 = mybir.dt.uint8
ALU = mybir.AluOpType
ACT = mybir.ActivationFunctionType
AX_X = mybir.AxisListType.X

P = 128
D = 1024
KD = D // P
TP = 512
DB, DS = 8, 8
TS = DB * DS
T = TP + TS
HT = T // 2
TPAD = TP + P
NC_ = DB + 1
PAST = 256
EPS = 1e-6

AH, ADK, ADV = 8, 128, 256
QKW, VW = AH * ADK, AH * ADV
CH = TP // P
LEVELS = (1, 2, 4, 8, 16, 32, 64)
XS = 8

BH, BHD = 12, 128
BW = BH * BHD
GH = 4
WINDOWS = ((128, 1), (512, 4), (2048, 16))
THETA = 10000.0
NEG = -1.0e30

HALF = 1024
RAWS = 3
SPLITS = 3
KVS = 5
TICKETS = 6


def perm(ap):
    return ap.rearrange("p (i q r) -> p r q i", q=4, r=4)


def constants():
    out = {"c_ident": np.eye(P, dtype=np.float32)}
    s, t = np.arange(P)[:, None], np.arange(P)[None, :]
    masks = [((s // (2 * L)) == (t // (2 * L))) & (s % (2 * L) < L) & (t % (2 * L) >= L) for L in LEVELS]
    out["c_levels"] = np.stack(masks, 1).astype(np.float32).reshape(P, -1)
    reset = np.ones((1, T), np.float32)
    reset[0, 0:TP:P] = 0
    reset[0, TP::DS] = 0
    out["c_reset"] = reset
    out["c_seq"] = (np.arange(TS)[:, None] // DS == np.arange(DB)[None, :]).astype(np.float32)
    q, i = np.arange(P) // 32, np.arange(P) % 32
    pos = np.empty((P, CH + 1), np.float32)
    for r in range(CH):
        pos[:, r] = 16 * i + 4 * q + r
    pos[:, CH] = PAST + np.arange(P) % DS
    half = BHD // 2
    inv = (np.float32(THETA) ** (-np.arange(half, dtype=np.float32) / np.float32(half))).astype(np.float32)
    ang = (pos[:, :, None] * inv).astype(np.float32)
    out["c_cos"], out["c_sin"] = np.cos(ang).astype(np.float32), np.sin(ang).astype(np.float32)
    f32 = lambda hidden: hidden.astype(np.float32)
    time = 16 * i + 4 * q
    dist = [time[:, None] - time[None, :] - diff for diff in range(1 - CH, CH)]
    out["c_mask0"] = np.concatenate([f32((d < 0) | (d > WINDOWS[0][0])) for d in dist], 1)
    later = time[None, :] > time[:, None]
    out["c_mask12"] = np.concatenate([f32(later), f32(later | (q[None, :] != q[:, None]))], 1)
    qb, qt = np.arange(TS) // DS, np.arange(TS) % DS
    parts = []
    for g, (window, dil) in enumerate(WINDOWS):
        dist = PAST + qt[:, None] - sample_keys(g)[None, :]
        parts.append(f32((dist % dil != 0) | (dist > window)))
        dist = qt[:, None] - qt[None, :]
        parts.append(f32((qb[:, None] != qb[None, :]) | (dist < 0) | (dist % dil != 0)))
    out["c_masks"] = np.concatenate(parts, 1)
    return out


def sample_keys(g):
    if g == 0:
        return PAST - 128 + np.arange(128)
    if g == 1:
        return np.arange(PAST)
    i, n = np.arange(P) // 16, np.arange(P) % 16
    return 16 * n + i


class Count:

    def __init__(self, eng, sem):
        self.eng, self.sem, self.n = eng, sem, 0

    def __call__(self, ins):
        self.n += 1
        ins.then_inc(self.sem, 1)
        self.eng.wait_ge(self.sem, self.n)


def program(nc, I, O):
    with ExitStack() as ctx:
        def sb(name, shape, dt=F32, stack=ctx):
            return stack.enter_context(nc.sbuf_tensor(name, shape, dt))

        def sem(name):
            return ctx.enter_context(nc.semaphore(name))


        raw = sb("raw", [P, RAWS, HALF])
        w_hi = sb("w_hi", [P, SPLITS, HALF], F32R)
        w_lo = sb("w_lo", [P, SPLITS, HALF], F32R)
        h_hi = sb("h_hi", [P, KD, TPAD], F32R)
        h_lo = sb("h_lo", [P, KD, TPAD], F32R)
        oz = sb("oz", [P, 2 * AH, T])
        ident = sb("ident", [P, P])
        ones = sb("ones", [P, P])
        eps = sb("eps", [P, 1])
        scT = sb("scT", [P, KD, NC_])
        ada = sb("ada", [P, 2, 3 * KD, NC_])
        adab = sb("adab", [P, 2, 3 * KD])
        normw = sb("normw", [P, 2, KD])
        amp = sb("amp", [P, KD, NC_])
        xpark = nc.dram_tensor("xpark", (P, KD * T), F32, kind="Internal").ap()

        PJ = ctx.enter_context(nc.psum_tensor("PJ", [P, 4, 512], F32))
        X = ctx.enter_context(nc.psum_tensor("X", [P, 4, 512], F32))
        ada_ps = PJ[:, 3, HT:HT + 3 * KD * NC_].rearrange("p (m n) -> p m n", n=NC_)

        s_const, s_x, s_c = sem("s_const"), sem("s_x"), sem("s_c")
        act_ch, dve_ch, pool_ch = sem("act_ch"), sem("dve_ch"), sem("pool_ch")
        raw_in = [sem(f"raw_in{i}") for i in range(RAWS)]
        raw_split = sem("raw_split")
        raw_used = sem("raw_used")
        hi_done = sem("hi_done")
        pj_ready = sem("pj_ready")
        pj_read = [sem("pj_read0"), sem("pj_read1")]
        ones_done, c_sig, c_silu, c_t, c_sb = (sem(x) for x in "ones_done c_sig c_silu c_t c_sb".split())
        x_t, x_sb = sem("x_t"), sem("x_sb")
        ada_done, amp_done = sem("ada_done"), sem("amp_done")
        n_sq, n_ms, n_r, n_xr, n_h, n_hi, n_lo = (sem(f"n_{x}") for x in "sq ms r xr h hi lo".split())
        parked, unparked = sem("parked"), sem("unparked")
        q_sig, z_sig, k_done, g_done, b_done, eb_done, dl_done, qe_done = (
            sem(x) for x in "q_sig z_sig k_done g_done b_done eb_done dl_done qe_done".split())
        sub_done, exp_done, lv_done = sem("sub_done"), sem("exp_done"), sem("lv_done")
        gram_ready, gram_read = sem("gram_ready"), sem("gram_read")
        kt_ready, kr_done, kz_done = sem("kt_ready"), sem("kr_done"), sem("kz_done")
        up_ready, up_read, os_ready, os_done = sem("up_ready"), sem("up_read"), sem("os_ready"), sem("os_done")
        ua_ready, ua_read, ub_ready, ub_read = sem("ua_ready"), sem("ua_read"), sem("ub_ready"), sem("ub_read")
        op_ready, sq_done, ms_ready, ms_read, r_done, fin_done = (
            sem(x) for x in "op_ready sq_done ms_ready ms_read r_done fin_done".split())
        s0_in, s0_out, sp_out = [sem("s0_in0"), sem("s0_in1")], [sem("s0_out0"), sem("s0_out1")], sem("sp_out")
        lb_in, lb_exp = sem("lb_in"), sem("lb_exp")
        a_const, tab_done = sem("a_const"), sem("tab_done")
        a_sq, a_rr, a_xn, a_rot, rows_done = (sem(x) for x in "a_sq a_rr a_xn a_rot rows_done".split())
        k_out, v_out = [sem("k_out0"), sem("k_out1")], sem("v_out")
        qkt_ready, qkt_read = sem("qkt_ready"), sem("qkt_read")
        za_sig, za_done = sem("za_sig"), sem("za_done")
        s_ready, s_mask, s_max, s_exp = sem("s_ready"), sem("s_mask"), sem("s_max"), sem("s_exp")
        c_in, w_exp, p_scaled = sem("c_in"), sem("w_exp"), sem("p_scaled")
        pt_ready, pt_read, o_ready, o_read = sem("pt_ready"), sem("pt_read"), sem("o_ready"), sem("o_read")
        kv_in = [sem(f"kv_in{i}") for i in range(KVS)]
        kc_t, kc_read, st_ready, st_read = sem("kc_t"), sem("kc_read"), sem("st_ready"), sem("st_read")
        ss_ready, ss_mask, ss_max, ss_exp = sem("ss_ready"), sem("ss_mask"), sem("ss_max"), sem("ss_exp")
        cs_in, ws_exp, ps_scaled = sem("cs_in"), sem("ws_exp"), sem("ps_scaled")
        pts_ready, pts_read, os1_ready, os1_read, vc_used = (
            sem(x) for x in "pts_ready pts_read os1_ready os1_read vc_used".split())
        parked1, unparked1, y_t, y_read = (sem(x) for x in "parked1 unparked1 y_t y_read".split())
        y_out = [sem("y_out0"), sem("y_out1")]
        n_hx = sem("n_hx")

        stream = []

        def cols(w, k0, nk, c0, width):
            return w[k0 * P:(k0 + nk) * P, c0:c0 + width].rearrange("(k p) c -> p k c", p=P)

        def piece(key, w, k0, nk, c0, width, freed):
            stream.append((key, cols(w, k0, nk, c0, width), nk, width, freed))

        aw, ow, adaw = I["a_w_in"][0], I["a_w_out"][0], I["ada_w"]
        count = {"split": 0, "used": 0}

        def split_piece(key, w, k0, nk, c0, width, ticket):
            count["split"] += 1
            split_no[key] = (count["split"] - 1, ticket)
            piece(key, w, k0, nk, c0, width, (raw_split, count["split"]))

        def used_piece(key, w, k0, nk, c0, width):
            count["used"] += 1
            piece(key, w, k0, nk, c0, width, (raw_used, count["used"]))

        split_no = {}

        def ada_piece(n):
            used_piece(("ada", n), adaw[n // 24], 0, KD, n % 24 * P, P)

        def ticket_w(h, t):
            return TICKETS * h + t

        for n in range(16):
            ada_piece(n)
        for h in range(AH):
            split_piece(("w", h, 0), aw, 0, KD, h * ADK, P, ticket_w(h, 0))
            split_piece(("w", h, 1), aw, 0, KD, QKW + h * ADK, P, ticket_w(h, 1))
            for kh in range(2):
                split_piece(("w", h, 2 + kh), aw, 4 * kh, 4, 2 * QKW + h * ADV, ADV, ticket_w(h, 3))
            for j in range(2):
                if j == 1:
                    for n in range(16 + 4 * h, 20 + 4 * h):
                        ada_piece(n)
                split_piece(("w", h, 4 + j), aw, 0, KD, 2 * QKW + VW + h * ADV + j * P, P, ticket_w(h, 4 + j))
        OUT0 = TICKETS * AH
        for m in range(KD):
            used_piece(("out0", m, 0), ow, 0, 8, m * P, P)
            piece(("out0", m, 1), ow, 8, 8, m * P, P, (pj_ready, OUT0 + m + 1))
        ATT0 = OUT0 + KD
        bw, bo = I["b_w_in"][0], I["b_w_out"][0]

        def pair_piece(key, k0, c0, c1, ticket):
            count["split"] += 1
            split_no[key] = (count["split"] - 1, ticket)
            w = bw.rearrange("(k p) (s c) -> p k s c", p=P, c=P)
            src = w[:, k0:k0 + 4, c0 // P:c1 // P + 1:(c1 - c0) // P, :]
            stream.append((key, src, 4, 2 * P, (raw_split, count["split"])))

        def ticket_a(j, t):
            return ATT0 + 12 * j + t

        for j in range(GH):
            for g in range(3):
                hd = (g * GH + j) * BHD
                for kk in range(2):
                    pair_piece(("a", j, 2 * g + kk), 4 * kk, hd, BW + hd, ticket_a(j, 2 * g + 1))
            for kk in range(2):
                pair_piece(("a", j, 6 + kk), 4 * kk, 2 * BW + (GH + j) * BHD, 2 * BW + (2 * GH + j) * BHD, ticket_a(j, 7))
            split_piece(("a", j, 8), bw, 0, KD, 2 * BW + j * BHD, P, ticket_a(j, 8))
            for g in range(3):
                split_piece(("a", j, 9 + g), bw, 0, KD, 3 * BW + (g * GH + j) * BHD, P, ticket_a(j, 9 + g))
        OUT1 = ATT0 + 12 * GH
        for m in range(KD):
            used_piece(("out1", m, 0), bo, 0, 6, m * P, P)
            piece(("out1", m, 1), bo, 6, 6, m * P, P, (pj_ready, OUT1 + m + 1))
        index = {x[0]: n for n, x in enumerate(stream)}
        split_keys = [x[0] for x in stream if x[0] in split_no]

        def loads_of(src):
            return 2 if len(src.shape) == 4 else 1

        def arrived(eng, key):
            n = index[key]
            eng.wait_ge(raw_in[n % RAWS], 16 * sum(loads_of(stream[x][1]) for x in range(n % RAWS, n + 1, RAWS)))

        def raw_of(key):
            n = index[key]
            nk, width = stream[n][2:4]
            return raw[:, n % RAWS, 0:nk * width].rearrange("p (k c) -> p k c", k=nk)

        def parts_of(key):
            i = split_no[key][0] % SPLITS
            nk = stream[index[key]][2]
            return [w[:, i, :].rearrange("p (k c) -> p k c", k=nk) for w in (w_hi, w_lo)]

        def split_hi(key):
            act = nc.scalar
            i = split_no[key][0]
            arrived(act, key)
            if i >= SPLITS:
                act.wait_ge(pj_ready, split_no[split_keys[i - SPLITS]][1] + 1)
            n = index[key]
            act.activation(w_hi[:, i % SPLITS, :], raw[:, n % RAWS, :], ACT.Copy).then_inc(hi_done, 1)

        def split_lo(key):
            dve = nc.vector
            i, n = split_no[key][0], index[key]
            dve.wait_ge(hi_done, i + 1)
            dve.tensor_tensor(w_lo[:, i % SPLITS, :], raw[:, n % RAWS, :], w_hi[:, i % SPLITS, :].bitcast(F32),
                              ALU.subtract).then_inc(raw_split, 1)

        def wait_read(eng, t):
            eng.wait_ge(pj_read[t % 2], t // 2 + 1)

        def begin(t):
            if t >= 2:
                wait_read(nc.tensor, t - 2)
            return t % 2

        def pj(t, n=HT):
            return PJ[:, 2 * (t % 2):2 * (t % 2) + 2, 0:n]

        def halves(ap):
            return ap.rearrange("p (e n) -> p e n", e=2)

        def project_T(t, key, cut=HT):
            nc.tensor.wait_ge(raw_split, split_no[key][0] + 1)
            s = begin(t)
            wh, wl = parts_of(key)
            for k in range(KD):
                for i, (a, b) in enumerate(((wh, h_hi), (wh, h_lo), (wl, h_hi))):
                    for e in range(2):
                        n0, n1 = (0, cut) if e == 0 else (cut, T)
                        last = nc.tensor.matmul(PJ[:, 2 * s + e, 0:n1 - n0], a[:, k, :], b[:, k, n0:n1],
                                                start=(k == 0 and i == 0), stop=(k == KD - 1 and i == 2))
            last.then_inc(pj_ready, 1)

        def project_rows(t, keys, tiles, out_of):
            for key in keys:
                nc.tensor.wait_ge(raw_split, split_no[key][0] + 1)
            begin(t)
            for tile in tiles:
                for k in range(KD):
                    wh, wl = parts_of(keys[k // 4])
                    for i, (a, b) in enumerate(((h_hi, wh), (h_lo, wh), (h_hi, wl))):
                        last = nc.tensor.matmul(out_of(tile), a[:, k, tile * P:(tile + 1) * P], b[:, k % 4, :],
                                                start=(k == 0 and i == 0), stop=(k == KD - 1 and i == 2))
            last.then_inc(pj_ready, 1)

        def project_ada(n, ready=None):
            key = ("ada", n)
            arrived(nc.tensor, key)
            w = raw_of(key)
            for k in range(KD):
                last = nc.tensor.matmul(ada_ps[:, n % 24, :], w[:, k, :], scT[:, k, :], start=(k == 0), stop=(k == KD - 1))
            last.then_inc(raw_used, 1)

        def read_ada(layer, m0, m1):
            nc.vector.tensor_tensor(ada[:, layer, m0:m1, :], ada_ps[:, m0:m1, :],
                                    adab[:, layer, m0:m1].unsqueeze(2).to_broadcast([P, m1 - m0, NC_]),
                                    ALU.add).then_inc(ada_done, 1)

        def make_amp(layer, chain):
            nc.vector.scalar_tensor_tensor(out=amp[:], in0=ada[:, layer, KD:2 * KD, :], scalar=1.0,
                                           in1=normw[:, layer, :].unsqueeze(2).to_broadcast([P, KD, NC_]),
                                           op0=ALU.add, op1=ALU.mult).then_inc(amp_done, 1)

        def norm_pe(layer, sq):
            pe = nc.tensor
            for k in range(KD):
                pe.wait_ge(n_sq, layer * KD + k + 1)
                for e in range(2):
                    last = pe.matmul(X[:, e, 0:HT], ones[:], sq[:, k % 2, e * HT:(e + 1) * HT],
                                     start=(k == 0), stop=(k == KD - 1))
                last.then_inc(n_ms, 1)

        def norm_act(layer, xT, sq, rn, xr, hf, chain, wait_x):
            act = nc.scalar
            for k in range(KD):
                wait_x(act, k)
                if k >= 2:
                    act.wait_ge(n_ms, layer * KD + k - 1)
                act.activation(sq[:, k % 2, :], xT[:, k, :], ACT.Square).then_inc(n_sq, 1)
            act.wait_ge(n_ms, (layer + 1) * KD)
            chain(act.activation(halves(rn[:]), X[:, 0:2, 0:HT], ACT.Ln, bias=eps[:, 0:1], scale=1.0 / D))
            act.activation(rn[:], rn[:], ACT.Exp, scale=-0.5).then_inc(n_r, 1)
            act.wait_ge(amp_done, layer + 1)
            for k in range(KD):
                act.wait_ge(n_xr, layer * KD + k + 1)
                if k >= 2:
                    act.wait_ge(n_lo, layer * KD + k - 1)
                act.activation(hf[:, k % 2, 0:TP], xr[:, k % 2, 0:TP], ACT.Identity,
                               scale=amp[:, k, 0:1], bias=ada[:, layer, k, 0:1]).then_inc(n_h, 1)
                act.wait_ge(n_h, layer * KD + k + 1)
                act.wait_ge(n_hi, layer * KD + k + 1)
                src = hf[:, k % 2, 0:TP]
                if layer:
                    chain(act.activation(h_hi[:, k, 0:TP].rearrange("p (r q i) -> p r q i", r=4, q=4), perm(src), ACT.Copy))
                else:
                    chain(act.activation(h_hi[:, k, 0:TP], src, ACT.Copy))
                act.activation(h_hi[:, k, TP:T], hf[:, k % 2, TP:T], ACT.Copy).then_inc(n_hx, 1)

        def norm_dve(layer, xT, rn, xr, hf, chain):
            dve = nc.vector

            def low(k):
                dve.wait_ge(n_hx, layer * KD + k + 1)
                src, dst, hi = hf[:, k % 2, 0:TP], h_lo[:, k, 0:TP], h_hi[:, k, 0:TP].bitcast(F32)
                if layer:
                    dst, hi = (x.rearrange("p (r q i) -> p r q i", r=4, q=4) for x in (dst, hi))
                    src = perm(src)
                chain(dve.tensor_tensor(dst, src, hi, ALU.subtract))
                dve.tensor_tensor(h_lo[:, k, TP:T], hf[:, k % 2, TP:T], h_hi[:, k, TP:T].bitcast(F32),
                                  ALU.subtract).then_inc(n_lo, 1)

            dve.wait_ge(n_r, layer + 1)
            for k in range(KD):
                if k >= 2:
                    dve.wait_ge(n_h, layer * KD + k - 1)
                dve.tensor_tensor(xr[:, k % 2, :], xT[:, k, :], rn[:], ALU.mult).then_inc(n_xr, 1)
                dve.wait_ge(n_xr, layer * KD + k + 1)
                if k >= 2:
                    dve.wait_ge(n_hx, layer * KD + k - 1)
                hs = hf[:, k % 2, TP:T].rearrange("p (b t) -> p b t", b=DB)
                xs = xr[:, k % 2, TP:T].rearrange("p (b t) -> p b t", b=DB)
                chain(dve.tensor_tensor(hs, xs, amp[:, k, 1:].unsqueeze(2).to_broadcast([P, DB, DS]), ALU.mult))
                dve.tensor_tensor(hs, hs, ada[:, layer, k, 1:].unsqueeze(2).to_broadcast([P, DB, DS]),
                                  ALU.add).then_inc(n_hi, 1)
                if k >= 1:
                    low(k - 1)
            low(KD - 1)

        ctx.enter_context(nc.allow_non_contiguous_dma("weights by feature block"))

        pro = ExitStack()
        xT = sb("xT0", [P, KD, T], stack=pro)
        c_row = sb("c_row", [NC_, D], stack=pro)
        c_sg = sb("c_sg", [NC_, D], stack=pro)
        nsq = sb("nsq", [P, 2, T], stack=pro)
        rn = sb("rn", [P, T], stack=pro)
        xr = sb("xr", [P, 2, T], stack=pro)
        hf = sb("hf", [P, 2, T], stack=pro)
        x_row = oz[:].rearrange("p a b -> p (a b)")[:, 0:5 * D].rearrange("p (t f) -> p t f", t=5)
        pro.close()

        st = ExitStack()
        lev = sb("lev", [P, len(LEVELS), P], U8, stack=st)
        reset = sb("reset", [P, T], stack=st)
        seqm = sb("seqm", [TS, DB], stack=st)
        lbr = sb("lbr", [P, 2, AH], stack=st)
        lb = sb("lb", [P, 2, AH], stack=st)
        bf = sb("bf", [P, AH], stack=st)
        gw = sb("gw", [P, 2], stack=st)
        q_ = sb("q_", [P, 2, T], stack=st)
        k_ = sb("k_", [P, 2, T], stack=st)
        b_ = sb("b_", [P, T], stack=st)
        qe = sb("qe", [P, 2, T], stack=st)
        fg = sb("fg", [P, T], stack=st)
        dl = sb("dl", [P, 2, CH + DB], stack=st)
        v_ = sb("v_", [P, 2, CH + 1, ADV], stack=st)
        s0 = sb("s0", [P, 2, DB, ADV], stack=st)
        sc = sb("sc", [P, CH, ADV], stack=st)
        kz = sb("kz", [TS, DB, ADK], stack=st)
        kr = sb("kr", [P, CH, ADK], stack=st)
        at = sb("at", [P, CH, P], stack=st)
        ats = sb("ats", [TS, TS], stack=st)
        qk = sb("qk", [P, len(LEVELS), T], stack=st)
        dd = sb("dd", [P, 2, T], stack=st)
        kh = sb("kh", [P, T], stack=st)
        sq0 = sb("sq0", [P, 2, T], stack=st)
        os_ = sb("os_", [P, 2, TS], stack=st)
        st.close()
        lev_raw = qk[:].rearrange("p l t -> p (l t)")[:, 0:len(LEVELS) * P]

        st1 = ExitStack()
        xT1 = sb("xT1", [P, KD, T], stack=st1)
        nsq1 = sb("nsq1", [P, 2, T], stack=st1)
        rn1 = sb("rn1", [P, T], stack=st1)
        xr1 = sb("xr1", [P, 2, T], stack=st1)
        hf1 = sb("hf1", [P, 2, T], stack=st1)
        yg = sb("yg", [P, 2, TS], stack=st1)
        st1.close()

        def blocks(ap, L):
            n = T if L <= 4 else TP
            return ap[:, 0:n].rearrange("p (n s l) -> p n s l", s=2, l=L)

        def pool_scan(pool, h):
            b = h % 2
            pool.wait_ge(dl_done, h + 1)
            wait_read(pool, ticket_w(h, 0))
            nc.gpsimd.tensor_tensor(qe[:, b], qe[:, b], q_[:, b], ALU.mult).then_inc(qe_done, 1)
            for i, L in enumerate(LEVELS):
                x = XS * h + i
                pool.wait_ge(exp_done, x + 1)
                if h >= 1:
                    pool.wait_ge(gram_ready, 8 * (h - 1) + i + 2)
                e, o = blocks(dd[:, x % 2], L), blocks(qk[:, i], L)
                nc.gpsimd.tensor_tensor(o[:, :, 0], blocks(k_[:, b], L)[:, :, 0], e[:, :, 0], ALU.mult)
                nc.gpsimd.tensor_tensor(o[:, :, 1], blocks(q_[:, b], L)[:, :, 1], e[:, :, 1], ALU.mult).then_inc(lv_done, 1)
            x = XS * h + 7
            pool.wait_ge(exp_done, x + 1)
            if h >= 1:
                pool.wait_ge(kt_ready, h)
            nc.gpsimd.tensor_tensor(kh[:], k_[:, b], dd[:, x % 2], ALU.mult).then_inc(lv_done, 1)

        def act_step(act, chain, h):
            b, g, f = h % 2, h - 1, h - 2
            new, scan, end = h < AH, 0 <= g < AH, 0 <= f

            def ahead(*pieces):
                for n in pieces:
                    hh, p = h + n // 6, n % 6
                    if hh < AH:
                        split_hi(("w", hh, p))

            if new:
                act.wait_ge(pj_ready, ticket_w(h, 0) + 1)
                if h >= 2:
                    act.wait_ge(lv_done, XS * (h - 1))
                act.activation(halves(q_[:, b]), pj(0), ACT.Sigmoid).then_inc(q_sig, 1)
                ahead(3)
            if end:
                act.wait_ge(ms_ready, f + 1)
                act.activation(sq0[:, 0, 0:TP], X[:, 0, :], ACT.Ln, bias=eps[:, 0:1], scale=1.0 / ADV)
                act.activation(sq0[:, 0, TP:T], X[:, 1, 0:TS], ACT.Ln, bias=eps[:, 0:1], scale=1.0 / ADV).then_inc(ms_read, 1)
                act.wait_ge(ms_read, f + 1)
                act.activation(sq0[:, 0, :], sq0[:, 0, :], ACT.Exp, scale=-0.5).then_inc(r_done, 1)
            if new:
                act.wait_ge(pj_ready, ticket_w(h, 1) + 1)
                if h >= 1:
                    act.wait_ge(b_done, h)
                act.activation(halves(fg[:]), pj(1), ACT.Sigmoid, bias=bf[:, h:h + 1]).then_inc(pj_read[1], 1)
                ahead(4)
                act.wait_ge(k_done, h + 1)
                act.activation(fg[:], fg[:], ACT.Ln).then_inc(g_done, 1)
                act.wait_ge(b_done, h + 1)
                act.activation(qe[:, b], b_[:], ACT.Exp).then_inc(eb_done, 1)
                for x in range(XS * h, XS * h + XS):
                    n = T if x % XS in (0, 1, 2, 7) else TP
                    act.wait_ge(sub_done, x + 1)
                    act.activation(dd[:, x % 2, 0:n], dd[:, x % 2, 0:n], ACT.Exp).then_inc(exp_done, 1)
                act.wait_ge(pj_ready, ticket_w(h, 2) + 1)
                act.activation(v_[:, b, 0:CH, :].rearrange("p c v -> p (c v)"),
                               PJ[:, 0:2, :].rearrange("p e n -> p (e n)"), ACT.Copy).then_inc(pj_read[0], 1)
            if scan:
                act.wait_ge(kt_ready, g + 1)
                act.activation(kr[:].rearrange("p c k -> p (c k)"), X[:, 3, :], ACT.Copy).then_inc(kr_done, 1)
                act.wait_ge(os_ready, g + 1)
                if g >= 1:
                    act.wait_ge(fin_done, 2 * g)
                act.activation(os_[:], X[:, 2, 384:512].rearrange("p (j t) -> p j t", j=2), ACT.Copy).then_inc(os_done, 1)
            if new:
                act.wait_ge(pj_ready, ticket_w(h, 3) + 1)
                act.activation(v_[0:TS, b, CH, :], PJ[0:TS, 2, 0:ADV], ACT.Copy).then_inc(pj_read[1], 1)
                ahead(5, 6)
                for j in range(2):
                    act.wait_ge(pj_ready, ticket_w(h, 4 + j) + 1)
                    act.activation(halves(oz[:, 2 * h + j, :]), pj(j), ACT.Sigmoid).then_inc(z_sig, 1)
                    ahead(7 + j)
            if scan:
                act.wait_ge(up_read, g + 1)
                act.dma_start(O["hgrn_prompt"][0, 0, g], sc[:, CH - 1, :]).then_inc(sp_out, 16)
                act.wait_ge(ub_read, g + 1)
                act.dma_start(O["hgrn_sample"][0, :, g].rearrange("b k v -> k b v"), s0[:, g % 2]).then_inc(s0_out[g % 2], 16)
                act.wait_ge(op_ready, g + 1)
                chain(act.activation(sq0[:, :, 0:TP], X[:, 2:4, :], ACT.Square))
                act.activation(sq0[:, :, TP:T], os_[:], ACT.Square).then_inc(sq_done, 1)


        def dve_gram(dve, chain, g, i):
            dve.wait_ge(gram_ready, 8 * g + i + 1)
            if i == 0 and g >= 1:
                dve.wait_ge(op_ready, g)
            for n in range(4 if i == 3 else 0):
                src = X[0:TS, 2, n * TS:(n + 1) * TS]
                if n == 0:
                    chain(dve.tensor_tensor(ats[:], src, ident[0:TS, 0:TS], ALU.mult))
                else:
                    chain(dve.copy_predicated(ats[:], lev[0:TS, n - 1, 0:TS], src))
            src = X[:, i % 2, :].rearrange("p (c t) -> p c t", c=CH)
            if i == 0:
                ins = dve.tensor_tensor(at[:], src, ident[:].unsqueeze(1).to_broadcast([P, CH, P]), ALU.mult)
            else:
                ins = dve.copy_predicated(at[:], lev[:, i - 1, :].unsqueeze(1).to_broadcast([P, CH, P]), src)
            ins.then_inc(gram_read, 1)
            dve.wait_ge(gram_read, 8 * g + i + 1)

        def dve_sub(dve, h, i):
            x = XS * h + i
            if x >= 2:
                dve.wait_ge(lv_done, x - 1)
            d = dd[:, x % 2]
            if i < 7:
                L = LEVELS[i]
                bb, o = blocks(b_[:], L), blocks(d, L)
                last = bb[:, :, 0, L - 1:L].to_broadcast([P, bb.shape[1], L])
                dve.tensor_tensor(o[:, :, 0], last, bb[:, :, 0], ALU.subtract)
                dve.tensor_tensor(o[:, :, 1], bb[:, :, 1], last, ALU.subtract).then_inc(sub_done, 1)
            else:
                for ap, o, n in ((b_[:, 0:TP], d[:, 0:TP], P), (b_[:, TP:T], d[:, TP:T], DS)):
                    bb, oo = (y.rearrange("p (c t) -> p c t", t=n) for y in (ap, o))
                    ins = dve.tensor_tensor(oo, bb[:, :, n - 1:n].to_broadcast([P, bb.shape[1], n]), bb, ALU.subtract)
                ins.then_inc(sub_done, 1)

        def dve_step(dve, chain, h):
            b, g, f = h % 2, h - 1, h - 2
            gb = g % 2
            new, scan, end = h < AH, 0 <= g < AH, 0 <= f

            def ahead(*pieces):
                for n in pieces:
                    hh, p = h + n // 6, n % 6
                    if hh < AH:
                        split_lo(("w", hh, p))

            def z_gate(j):
                dve.wait_ge(z_sig, 2 * h + j + 1)
                dve.tensor_tensor(halves(oz[:, 2 * h + j, :]), pj(j), halves(oz[:, 2 * h + j, :]),
                                  ALU.mult).then_inc(pj_read[j], 1)

            if new:
                dve.wait_ge(q_sig, h + 1)
                dve.tensor_tensor(halves(q_[:, b]), pj(0), halves(q_[:, b]), ALU.mult).then_inc(pj_read[0], 1)
                ahead(3)
            if end:
                dve.wait_ge(r_done, f + 1)
                for j in range(2):
                    dve.scalar_tensor_tensor(out=sq0[:, 1, 0:TP], in0=X[:, 2 + j, :], scalar=gw[:, j:j + 1],
                                             in1=sq0[:, 0, 0:TP], op0=ALU.mult, op1=ALU.mult)
                    chain(dve.scalar_tensor_tensor(out=sq0[:, 1, TP:T], in0=os_[:, j], scalar=gw[:, j:j + 1],
                                                   in1=sq0[:, 0, TP:T], op0=ALU.mult, op1=ALU.mult))
                    dve.tensor_tensor(oz[:, 2 * f + j], oz[:, 2 * f + j], sq0[:, 1], ALU.mult).then_inc(fin_done, 1)
                    dve.wait_ge(fin_done, 2 * f + j + 1)
            if new:
                ahead(4)
                wait_read(dve, ticket_w(h, 1))
                chain(dve.tensor_scalar(fg[:], fg[:], lb[:, 1, h:h + 1], lb[:, 0, h:h + 1], ALU.mult, ALU.add))
                if h >= 2:
                    dve.wait_ge(lv_done, XS * (h - 1))
                dve.tensor_scalar(k_[:, b], fg[:], -1.0, 1.0, ALU.mult, ALU.add).then_inc(k_done, 1)
            grams = iter(range(8 if scan else 0))

            def gram():
                for i in grams:
                    dve_gram(dve, chain, g, i)
                    break

            gram()
            gram()
            if new:
                dve.wait_ge(g_done, h + 1)
                dve.tensor_tensor_scan(b_[:], reset[:], fg[:], 0.0, ALU.mult, ALU.add).then_inc(b_done, 1)
                dve.wait_ge(b_done, h + 1)
                for i in range(8):
                    gram()
                    dve_sub(dve, h, i)
                    if i == 1:
                        dve.wait_ge(eb_done, h + 1)
                        dve.tensor_copy(dl[:, b, 0:CH], qe[:, b, P - 1:TP:P])
                        dve.tensor_copy(dl[:, b, CH:], qe[:, b, TP + DS - 1:T:DS]).then_inc(dl_done, 1)
            for _ in range(8):
                gram()
            if scan:
                dve.wait_ge(kt_ready, g + 1)
                dve.tensor_tensor(kz[:], X[0:TS, 2, 256:384].unsqueeze(1).to_broadcast([TS, DB, ADK]),
                                  seqm[:].unsqueeze(2).to_broadcast([TS, DB, ADK]), ALU.mult).then_inc(kz_done, 1)
                dve.wait_ge(up_ready, g + 1)
                if g >= 1:
                    dve.wait_ge(sp_out, 16 * g)
                chain(dve.tensor_copy(sc[:, 0], X[:, 0, 0:ADV]))
                for c in range(1, CH):
                    ins = dve.scalar_tensor_tensor(out=sc[:, c], in0=sc[:, c - 1], scalar=dl[:, gb, c:c + 1],
                                                   in1=X[:, c // 2, c % 2 * ADV:(c % 2 + 1) * ADV],
                                                   op0=ALU.mult, op1=ALU.add)
                    if c < CH - 1:
                        chain(ins)
                ins.then_inc(up_read, 1)
            if new:
                ahead(5, 6)
                z_gate(0)
                ahead(7)

            def new_states(b0, ready, bank, read):
                dve.wait_ge(ready, g + 1)
                for i in range(4):
                    ins = dve.scalar_tensor_tensor(out=s0[:, gb, b0 + i], in0=s0[:, gb, b0 + i],
                                                   scalar=dl[:, gb, CH + b0 + i:CH + b0 + i + 1],
                                                   in1=X[:, bank + i // 2, i % 2 * ADV:(i % 2 + 1) * ADV],
                                                   op0=ALU.mult, op1=ALU.add)
                ins.then_inc(read, 1)

            if scan:
                new_states(0, ua_ready, 2, ua_read)
            if new:
                if h == 1:
                    dve.wait_ge(raw_used, 24)
                    dve.wait_ge(z_sig, 2 * h + 2)
                    read_ada(0, 16, 24)
                if h == AH - 1:
                    dve.wait_ge(raw_used, 48)
                    dve.wait_ge(z_sig, 2 * h + 2)
                    read_ada(1, 0, 3 * KD)
                z_gate(1)
                ahead(8)
            if scan:
                new_states(4, ub_ready, 0, ub_read)

        def dve_residual(dve, chain, layer, t, m, xT, yg):
            s = t % 2
            dve.wait_ge(pj_ready, t + 1)
            gate = ada[:, layer, 2 * KD + m, 0:1]
            y, ys, x = PJ[:, 2 * s, :], PJ[:, 2 * s + 1, 0:TS], xT[:, m, 0:TP]
            pairs = [(y, x)]
            if layer:
                y = y.rearrange("p (r q i) -> p r q i", r=4, q=4)
                pairs = [(y[:, r], perm(x)[:, r]) for r in range(4)]
            for y, x in pairs:
                dve.scalar_tensor_tensor(out=x, in0=y, scalar=gate, in1=x, op0=ALU.mult, op1=ALU.add)
            seqs = lambda ap: ap.rearrange("p (b t) -> p b t", b=DB)
            chain(dve.tensor_tensor(seqs(yg[:, s]), seqs(ys),
                                    ada[:, layer, 2 * KD + m, 1:].unsqueeze(2).to_broadcast([P, DB, DS]), ALU.mult))
            dve.tensor_tensor(xT[:, m, TP:T], xT[:, m, TP:T], yg[:, s], ALU.add).then_inc(pj_read[s], 1)

        def pe_grams(pe, g):
            b = g % 2
            for i in range(8):
                pe.wait_ge(lv_done, XS * g + i)
                if i == 0:
                    pe.wait_ge(k_done, g + 1)
                    wait_read(pe, ticket_w(g, 0))
                    if g >= 1:
                        pe.wait_ge(ms_read, g)
                        pe.wait_ge(fin_done, 2 * g)
                if i >= 2:
                    pe.wait_ge(gram_read, 8 * g + i - 1)
                pair = lambda n: (k_[:, b], q_[:, b]) if n == 0 else (qk[:, n - 1], qk[:, n - 1])
                left, right = pair(i)
                for n in range(4 if i == 3 else 0):
                    pe.matmul(X[0:TS, 2, n * TS:(n + 1) * TS], pair(n)[0][:, TP:T], pair(n)[1][:, TP:T],
                              start=True, stop=True)
                for c in range(CH):
                    last = pe.matmul(X[:, i % 2, c * P:(c + 1) * P], left[:, c * P:(c + 1) * P],
                                     right[:, c * P:(c + 1) * P], start=True, stop=True)
                last.then_inc(gram_ready, 1)

        def pe_states(pe, g):
            b = g % 2
            pe.wait_ge(lv_done, XS * g + XS)
            pe.wait_ge(gram_read, 8 * g + 8)
            for c in range(CH):
                pe.transpose(X[:, 3, c * P:(c + 1) * P], kh[:, c * P:(c + 1) * P], ident[:])
            pe.transpose(X[0:TS, 2, 256:384], kh[:, TP:T], ident[:]).then_inc(kt_ready, 1)
            wait_read(pe, ticket_w(g, 3))
            wait_read(pe, ticket_w(g, 2))
            pe.wait_ge(s0_in[b], 16 * (g // 2 + 1))
            pe.wait_ge(qe_done, g + 1)
            pe.wait_ge(kz_done, g + 1)
            for j in range(2):
                c0 = 384 + j * TS
                pe.matmul(X[:, 2, c0:c0 + TS], v_[0:TS, b, CH, j * P:(j + 1) * P], ats[:], start=True, stop=False)
                for n in range(DB):
                    last = pe.matmul(X[:, 2, c0 + n * DS:c0 + (n + 1) * DS], s0[:, b, n, j * P:(j + 1) * P],
                                     qe[:, b, TP + n * DS:TP + (n + 1) * DS], start=False, stop=(n == DB - 1))
            last.then_inc(os_ready, 1)
            pe.wait_ge(kr_done, g + 1)
            for c in range(CH):
                last = pe.matmul(X[:, c // 2, c % 2 * ADV:(c % 2 + 1) * ADV], kr[:, c], v_[:, b, c], start=True, stop=True)
            last.then_inc(up_ready, 1)

        def pe_new_states(pe, g, b0, bank, ready):
            for i in range(4):
                last = pe.matmul(X[:, bank + i // 2, i % 2 * ADV:(i % 2 + 1) * ADV], kz[:, b0 + i],
                                 v_[0:TS, g % 2, CH], start=True, stop=True)
            last.then_inc(ready, 1)

        def pe_step(pe, h):
            b, g, f = h % 2, h - 1, h - 2
            new, scan, end = h < AH, 0 <= g < AH, 0 <= f
            if new:
                project_T(ticket_w(h, 0), ("w", h, 0))
            if end:
                pe.wait_ge(sq_done, f + 1)
                pe.wait_ge(ub_read, f + 1)
                for bank, a, z in ((0, 0, TP), (1, TP, T)):
                    for j in range(2):
                        last = pe.matmul(X[:, bank, 0:z - a], ones[:], sq0[:, j, a:z], start=(j == 0), stop=(j == 1))
                last.then_inc(ms_ready, 1)
            if new:
                project_T(ticket_w(h, 1), ("w", h, 1))
            if scan:
                pe_grams(pe, g)
            keys = [("w", h, 2), ("w", h, 3)]
            if new:
                project_rows(ticket_w(h, 2), keys, range(CH),
                             lambda c: PJ[:, c // 2, c % 2 * ADV:(c % 2 + 1) * ADV])
                wait_read(pe, ticket_w(h, 1))
                for n in range(16 + 4 * h, 20 + 4 * h):
                    if n == 40:
                        pe.wait_ge(ada_done, 2)
                    project_ada(n)
            if scan:
                pe_states(pe, g)
            if new:
                project_rows(ticket_w(h, 3), keys, [CH], lambda c: PJ[:, 2, 0:ADV])
                project_T(ticket_w(h, 4), ("w", h, 4))
            if scan:
                pe.wait_ge(os_done, g + 1)
                pe_new_states(pe, g, 0, 2, ua_ready)
            if new:
                project_T(ticket_w(h, 5), ("w", h, 5))
            if scan:
                pe.wait_ge(up_read, g + 1)
                pe_new_states(pe, g, 4, 0, ub_ready)
                pe.wait_ge(ua_read, g + 1)
                for j in range(2):
                    for c in range(CH):
                        out = X[:, 2 + j, c * P:(c + 1) * P]
                        last = pe.matmul(out, v_[:, g % 2, c, j * P:(j + 1) * P], at[:, c], start=True, stop=(c == 0))
                        if c:
                            last = pe.matmul(out, sc[:, c - 1, j * P:(j + 1) * P], qe[:, g % 2, c * P:(c + 1) * P],
                                             start=False, stop=True)
                last.then_inc(op_ready, 1)

        def pe_out(pe, name, t0, nk, then=None):
            for m in range(KD):
                begin(t0 + m)
                for n in range(2 * nk):
                    if n % nk == 0:
                        arrived(pe, (name, m, n // nk))
                    w = raw_of((name, m, n // nk))
                    for e, (a, z) in enumerate(((0, TP), (TP, T))):
                        last = pe.matmul(PJ[:, 2 * ((t0 + m) % 2) + e, 0:z - a], w[:, n % nk, :],
                                         oz[:, n, a:z], start=(n == 0), stop=(n == 2 * nk - 1))
                    if n == nk - 1:
                        last.then_inc(raw_used, 1)
                last.then_inc(pj_ready, 1)
                if then:
                    then(m)

        st2 = ExitStack()
        tail = oz[:].rearrange("p a b -> p (a b)")[:, BH * T:]
        tail_at = [0]

        def in_tail(*shape):
            n = int(np.prod(shape))
            ap = tail[:, tail_at[0]:tail_at[0] + n]
            tail_at[0] += n
            assert tail_at[0] <= (2 * AH - BH) * T
            names = "abcd"[:len(shape)]
            return ap.rearrange(f"p ({' '.join(names)}) -> p {' '.join(names)}", **dict(zip(names, shape))) \
                if len(shape) > 1 else ap

        tcos = sb("tcos", [P, CH + 1, 2, BHD], stack=st2)
        tsin = sb("tsin", [P, CH + 1, 2, BHD], stack=st2)
        ra = sb("ra", [P, 2, 2 * 2 * BHD], stack=st2)
        rb = sb("rb", [P, 2 * 2 * BHD], stack=st2)
        rows = sb("rows", [P, 2, CH + 1, 2, BHD], stack=st2)
        qkT = sb("qkT", [P, 3, 2, T], stack=st2)
        vr = sb("vr", [P, 3, CH + 1, BHD], stack=st2)
        p0 = sb("p0", [P, CH, TP], stack=st2)
        p12 = sb("p12", [P, 2, CH, P], stack=st2)
        pt = sb("pt", [P, CH, TP], stack=st2)
        kvc = sb("kvc", [P, KVS, DB, BHD], stack=st2)
        kcT = sb("kcT", [P, DB, P], stack=st2)
        m0 = sb("m0", [P, 2 * CH - 1, P], U8, stack=st2)
        m12 = sb("m12", [P, 2, P], U8, stack=st2)
        MS = 4 * P + 3 * TS
        ps_ = in_tail(MS)
        ms_ = in_tail(MS // 4).bitcast(U8)[0:TS]
        zs = in_tail(T)
        sts = in_tail(4, TS)
        pts = in_tail(7, TS)
        nm, sm, wx, cx = (in_tail(3, CH) for _ in range(4))
        mn, den = in_tail(CH), in_tail(CH)
        nms, sms, wxs, cxs = (in_tail(3) for _ in range(4))
        mns, dens = in_tail(1), in_tail(1)
        ssum, rr = in_tail(2, 4), in_tail(2, 4)
        st2.close()
        qkw = pts.rearrange("p a b -> p (a b)")[:, 0:2 * BHD].rearrange("p (s c) -> p s c", s=2)
        cs_raw = rows[:].rearrange("p a b c d -> p (a b c d)")[:, 0:2 * (CH + 1) * 64].rearrange(
            "p (s t c) -> p s t c", s=2, t=CH + 1)
        masks_raw = p0[:].rearrange("p r k -> p (r k)")
        n0, n12 = (2 * CH - 1) * P, 2 * P
        masks = ((m0[:].rearrange("p d k -> p (d k)"), masks_raw[:, 0:n0], I["c_mask0"]),
                 (m12[:].rearrange("p g k -> p (g k)"), masks_raw[:, n0:n0 + n12], I["c_mask12"]),
                 (ms_, masks_raw[0:TS, n0 + n12:n0 + n12 + MS], I["c_masks"]))
        xpark1 = nc.dram_tensor("xpark1", (P, KD * T), F32, kind="Internal").ap()

        st3 = ExitStack()
        xT2 = sb("xT2", [P, KD, T], stack=st3)
        yg2 = sb("yg2", [P, 2, TS], stack=st3)
        yr = sb("yr", [P, 2, CH + 1, P], stack=st3)
        st3.close()

        SCALE = BHD ** -0.5
        CACHES = ("cache_kv_w128", "cache_kv_w512", "cache_kv_w512", "cache_kv_w2048")
        TILE_AT = (0, TP - 320, TP - 192, TP)
        SEG = (0, 192, 512, MS)
        GROUP_OF = (0, 1, 1, 2)
        kv_total, kv_count = [], [0] * KVS

        def kv_tile(j, i):
            return (8 * j + i) % KVS

        def kv_load(sp, j, i):
            m, n, side = 8 * j + i, i % 4, i // 4
            if m >= KVS:
                jj, ii = divmod(m - KVS, 8)
                sp.wait_ge(*((kc_t, 4 * jj + ii + 1) if ii < 4 else (vc_used, jj + 1)))
            slot = m % KVS
            src = I[CACHES[n]][0, :, :, side, j, :].rearrange("b k c -> k b c")
            if n == 3:
                parts = [(kvc[16 * x:16 * x + 16, slot], src[x:PAST:16]) for x in range(DS)]
            else:
                k0 = P * (n == 2)
                parts = [(kvc[:, slot], src[k0:k0 + P])]
            for dst, ap in parts:
                sp.dma_start(dst, ap).then_inc(kv_in[slot], 16)

        def kv_value(j, i):
            m = 8 * j + i
            return 16 * sum(DS if x % 4 == 3 else 1 for x in range(m % KVS, m + 1, KVS))

        def store_rows(sp, side, g, j, tiles, done):
            name = ("kv128", "kv512", "kv2048")[g]
            out = O[name + "_prompt"][0, 0, :, side, j, :]
            i0 = 24 if g == 0 else 0
            out = out.rearrange("(i q r) c -> q i r c", q=4, r=4)
            for x in range(4):
                sp.dma_start(out[x], tiles[32 * x + i0:32 * x + 32, 0:CH, :]).then_inc(done, 16)
            out = O[name + "_sample"][0, :, :, side, j, :].rearrange("b t c -> (b t) c")
            sp.dma_start(out, tiles[0:TS, CH, :]).then_inc(done, 16)

        def store_k(sp, j, g):
            w = 3 * j + g
            sp.wait_ge(rows_done, 3 * w + 3)
            store_rows(sp, 0, g, j, rows[:, w % 2, :, 1, :], k_out[w % 2])

        def store_v(sp, j):
            sp.wait_ge(pj_read[0], (ticket_a(j, 8)) // 2 + 1)
            sp.wait_ge(pj_read[1], (ticket_a(j, 7)) // 2 + 1)
            for g in range(3):
                store_rows(sp, 1, g, j, vr[:, g], v_out)

        after = {}

        def at_piece(key, ahead, what, *args):
            after.setdefault(index[key] + ahead, []).append((what, args))

        for j in range(GH):
            for g in range(3):
                at_piece(("a", j, 7 + 2 * g), 0, store_k, j, g)
            if j == 0:
                at_piece(("a", j, 5), 0, kv_load, j, 0)
            for i in range(1, 5):
                at_piece(("a", j, 11), 0, kv_load, j, i)
            for i in range(5, 8):
                at_piece(("a", j, 11), min(i - 2, 5) if j < GH - 1 else 3, kv_load, j, i)
            if j < GH - 1:
                at_piece(("a", j, 11), 6, kv_load, j + 1, 0)
            at_piece(("a", j, 11), 3, store_v, j)

        def chunk(c):
            return ((0, 2, P, 0), (2, 2, P, 1), (CH, 1, TS, 2))[c]

        def chunk_in(c):
            t0, n, p, bank = chunk(c)
            return PJ[0:p, bank, 0:n * 256].rearrange("p (t s c) -> p t s c", t=n, s=2)

        def rope_act(act, chain, j, g, c):
            t0, n, p, bank = chunk(c)
            u = 9 * j + 3 * g + c
            act.wait_ge(pj_ready, ticket_a(j, 2 * g + c // 2) + 1)
            if u >= 2:
                act.wait_ge(rows_done, u - 1)
            for x in range(2 * n):
                ins = act.activation(ra[0:p, u % 2, x * BHD:(x + 1) * BHD],
                                     PJ[0:p, bank, x * BHD:(x + 1) * BHD], ACT.Square,
                                     accum_out=ssum[0:p, u % 2, x:x + 1])
            chain(ins)
            chain(act.activation(rr[0:p, u % 2, 0:2 * n], ssum[0:p, u % 2, 0:2 * n], ACT.Ln, bias=eps[0:p, 0:1],
                                 scale=1.0 / BHD))
            act.activation(rr[0:p, u % 2, 0:2 * n], rr[0:p, u % 2, 0:2 * n], ACT.Exp, scale=-0.5).then_inc(a_rr, 1)

        def rope_dve(dve, chain, j, g, c):
            t0, n, p, bank = chunk(c)
            u, w = 9 * j + 3 * g + c, 3 * j + g
            dve.wait_ge(a_rr, u + 1)
            if u >= 1:
                dve.wait_ge(a_rot, u)
            xn = rb[0:p, 0:n * 256].rearrange("p (t s c) -> p t s c", t=n, s=2)
            done = (a_xn, pj_read[0], pj_read[1])[c]
            dve.tensor_tensor(xn, chunk_in(c), rr[0:p, u % 2, 0:2 * n].rearrange("p (t s) -> p t s", t=n)
                              .unsqueeze(3).to_broadcast([p, n, 2, BHD]), ALU.mult).then_inc(done, 1)
            wait_xn(dve, j, g, c)
            if c == 0 and w >= 2:
                dve.wait_ge(qkt_ready, w - 1)
                dve.wait_ge(k_out[w % 2], 80 * (w // 2))
            dst = rows[0:p, w % 2, t0:t0 + n]
            chain(dve.tensor_tensor(dst, xn, tcos[0:p, t0:t0 + n], ALU.mult))
            dve.wait_ge(a_rot, u + 1)
            dve.tensor_tensor(dst, dst, ra[0:p, u % 2, 0:n * 256].rearrange("p (t s c) -> p t s c", t=n, s=2),
                              ALU.add).then_inc(rows_done, 1)

        def wait_xn(eng, j, g, c):
            if c == 0:
                eng.wait_ge(a_xn, 3 * j + g + 1)
            else:
                wait_read(eng, ticket_a(j, 2 * g + c - 1))

        def rope_pool(pool, j, g, c):
            t0, n, p, bank = chunk(c)
            u = 9 * j + 3 * g + c
            wait_xn(pool, j, g, c)
            h = BHD // 2
            src = rb[0:p, 0:n * 256].rearrange("p (t h c) -> p t h c", t=2 * n, h=2)
            dst = ra[0:p, u % 2, 0:n * 256].rearrange("p (t h c) -> p t h c", t=2 * n, h=2)
            tab = tsin[0:p, t0:t0 + n].rearrange("p t s (h c) -> p (t s) h c", h=2)
            nc.gpsimd.tensor_tensor(dst[:, :, 0], src[:, :, 1], tab[:, :, 0], ALU.mult)
            nc.gpsimd.tensor_tensor(dst[:, :, 1], src[:, :, 0], tab[:, :, 1], ALU.mult).then_inc(a_rot, 1)

        def pe_qk_rows(pe, j, t):
            keys = [("a", j, 2 * (t // 2)), ("a", j, 2 * (t // 2) + 1)]
            if t % 2 == 0:
                project_rows(ticket_a(j, t), keys, range(CH), lambda c: PJ[:, c // 2, c % 2 * 256:c % 2 * 256 + 256])
            else:
                project_rows(ticket_a(j, t), keys, [CH], lambda c: PJ[:, 2, 0:256])

        def pe_v0_rows(pe, j):
            key = ("a", j, 8)
            pe.wait_ge(raw_split, split_no[key][0] + 1)
            begin(ticket_a(j, 8))
            wh, wl = parts_of(key)
            for tile in range(CH + 1):
                for k in range(KD):
                    for i, (a, b) in enumerate(((h_hi, wh), (h_lo, wh), (h_hi, wl))):
                        last = pe.matmul(PJ[:, tile // CH, tile % CH * P:tile % CH * P + P], a[:, k, tile * P:(tile + 1) * P],
                                         b[:, k, :], start=(k == 0 and i == 0), stop=(k == KD - 1 and i == 2))
            last.then_inc(pj_ready, 1)

        def pe_qkt(pe, j, g):
            w = 3 * j + g
            pe.wait_ge(rows_done, 3 * w + 3)
            if g == 0 and j:
                pe.wait_ge(pt_read, 3 * (j - 1) + 2)
                pe.wait_ge(st_read, 4 * j)
            if g == 1 and j:
                pe.wait_ge(pt_read, 3 * j)
                pe.wait_ge(pts_read, j)
            if w:
                pe.wait_ge(qkt_read, w)
            for s in range(2):
                for t in range(CH):
                    pe.transpose(X[:, s, t * P:(t + 1) * P], rows[:, w % 2, t, s, :], ident[:])
                last = pe.transpose(X[:, 2, s * TS:(s + 1) * TS], rows[0:TS, w % 2, CH, s, :], ident[0:TS, 0:TS])
            last.then_inc(qkt_ready, 1)

        def pe_s0(pe, j):
            pe.wait_ge(kc_read, 4 * j + 1)
            pe.wait_ge(st_read, 4 * j + 1)
            if j:
                pe.wait_ge(os1_read, j)
            for r in range(CH):
                last = pe.matmul(X[:, r, :], qkT[:, 0, 0, r * P:(r + 1) * P], qkT[:, 0, 1, 0:TP], start=True, stop=True)
            last.then_inc(s_ready, 1)

        def pe_s12(pe, j):
            pe.wait_ge(s_mask, 3 * j + 1)
            for g in (1, 2):
                for r in range(CH):
                    last = pe.matmul(X[:, 1 + g, r * P:(r + 1) * P], qkT[:, g, 0, r * P:(r + 1) * P],
                                     qkT[:, g, 1, r * P:(r + 1) * P], start=True, stop=True)
                last.then_inc(s_ready, 1)

        def pe_kt(pe, j, n):
            pe.wait_ge(kv_in[kv_tile(j, n)], kv_value(j, n))
            if n == 0:
                pe.wait_ge(qkt_read, 3 * j + 3)
            else:
                pe.wait_ge(kc_read, 4 * j + n)
            if n == 1:
                pe.wait_ge(s_mask, 3 * j + 1)
            for b in range(DB):
                last = pe.transpose(X[:, b // 4, b % 4 * P:(b % 4 + 1) * P], kvc[:, kv_tile(j, n), b, :], ident[:])
            last.then_inc(kc_t, 1)

        def pe_st(pe, j, n):
            g = GROUP_OF[n]
            pe.wait_ge(kc_read, 4 * j + n + 1)
            if n == 0:
                pe.wait_ge(qkt_read, 3 * j + 3)
            else:
                pe.wait_ge(st_read, 4 * j + n)
            if n == 1:
                pe.wait_ge(s_mask, 3 * j + 2)
            for b in range(DB):
                last = pe.matmul(X[:, 2, n * TS + b * DS:n * TS + (b + 1) * DS], kcT[:, b, :],
                                 qkT[:, g, 0, TP + b * DS:TP + (b + 1) * DS], start=True, stop=True)
            last.then_inc(st_ready, 1)

        def pe_sfin(pe, j, g):
            tiles = [n for n in range(4) if GROUP_OF[n] == g]
            pe.wait_ge(st_read, 4 * j + tiles[-1] + 1)
            if g == 0:
                pe.wait_ge(s_mask, 3 * j + 3)
            else:
                pe.wait_ge(ss_mask, 3 * j + g)
            for x, n in enumerate(tiles):
                pe.transpose(X[0:TS, 3, x * P:(x + 1) * P], sts[:, n, :], ident[:])
            x = len(tiles) * P
            pe.matmul(X[0:TS, 3, x:x + TS], qkT[:, g, 0, TP:T], qkT[:, g, 1, TP:T], start=True,
                      stop=True).then_inc(ss_ready, 1)

        def pe_pt0(pe, a, half):
            if half == 0:
                pe.wait_ge(p_scaled, 2 * a + 1)
                pe.wait_ge(kc_read, 4 * a + 4)
            else:
                pe.wait_ge(pt_read, 3 * a + 1)
            for k in range(2):
                for r in range(CH):
                    k0 = (2 * half + k) * P
                    last = pe.transpose(X[:, k, r * P:(r + 1) * P], p0[:, r, k0:k0 + P], ident[:])
            last.then_inc(pt_ready, 1)

        def pe_pt12(pe, a, j):
            pe.wait_ge(p_scaled, 2 * a + 2)
            pe.wait_ge(pt_read, 3 * a + 2)
            if j < GH:
                pe.wait_ge(qkt_read, 3 * j + 1)
            for g in range(2):
                for r in range(CH):
                    last = pe.transpose(X[:, g, r * P:(r + 1) * P], p12[:, g, r, :], ident[:])
            last.then_inc(pt_ready, 1)

        def pe_pts(pe, a, j):
            pe.wait_ge(ps_scaled, a + 1)
            pe.wait_ge(st_read, 4 * a + 4)
            if j < GH:
                pe.wait_ge(qkt_read, 3 * j + 1)
            for n in range(4):
                pe.transpose(X[:, 2, n * TS:(n + 1) * TS], ps_[0:TS, TILE_AT[n]:TILE_AT[n] + P], ident[0:TS, 0:TS])
            for g in range(3):
                c0 = SEG[g + 1] - TS
                last = pe.transpose(X[0:TS, 2, (4 + g) * TS:(5 + g) * TS], ps_[0:TS, c0:c0 + TS], ident[0:TS, 0:TS])
            last.then_inc(pts_ready, 1)

        def pe_m(pe, a, g):
            if g == 0:
                pe.wait_ge(pt_read, 3 * a + 2)
                pe.wait_ge(ss_mask, 3 * a + 3)
                for k in range(CH):
                    last = pe.matmul(X[:, 3, :], vr[:, 0, k, :], pt[:, k, :], start=(k == 0), stop=(k == CH - 1))
            else:
                pe.wait_ge(pt_read, 3 * a + 3)
                pe.wait_ge(o_read, 3 * a + g)
                for r in range(CH):
                    last = pe.matmul(X[:, 3, r * P:(r + 1) * P], vr[:, g, r, :], pt[:, g - 1, r * P:(r + 1) * P],
                                     start=True, stop=True)
            last.then_inc(o_ready, 1)

        def pe_ms(pe, a):
            pe.wait_ge(o_read, 3 * a + 3)
            pe.wait_ge(pts_read, a + 1)
            for i in range(4, 8):
                pe.wait_ge(kv_in[kv_tile(a, i)], kv_value(a, i))
            for g in range(3):
                pe.matmul(X[:, 3, g * TS:(g + 1) * TS], vr[0:TS, g, CH, :], pts[0:TS, 4 + g, :], start=True, stop=False)
                tiles = [n for n in range(4) if GROUP_OF[n] == g]
                for n in tiles:
                    for b in range(DB):
                        c0 = g * TS + b * DS
                        last = pe.matmul(X[:, 3, c0:c0 + DS], kvc[:, kv_tile(a, 4 + n), b, :],
                                         pts[:, n, b * DS:(b + 1) * DS], start=False,
                                         stop=(n == tiles[-1] and b == DB - 1))
            last.then_inc(vc_used, 1)

        def pe_attention(pe, j):
            a, new, old = j - 1, j < GH, j > 0
            for k in range(12 if new else 8):
                if new:
                    if k < 8:
                        pe_qk_rows(pe, j, k)
                    elif k == 8:
                        pe_v0_rows(pe, j)
                    else:
                        project_T(ticket_a(j, k), ("a", j, k))
                if old:
                    if k == 0:
                        pe_st(pe, a, 3)
                        pe_sfin(pe, a, 1)
                    if k == 1:
                        pe_sfin(pe, a, 2)
                        pe_pt0(pe, a, 0)
                    if k == 2:
                        pe_pt0(pe, a, 1)
                    if k == 3:
                        pe_m(pe, a, 0)
                if new and k == 3:
                    pe_qkt(pe, j, 0)
                if old:
                    if k == 4:
                        pe_pt12(pe, a, j)
                        pe_pts(pe, a, j)
                    if k == 5:
                        pe_m(pe, a, 1)
                if new and k == 5:
                    pe_qkt(pe, j, 1)
                if old and k == 6:
                    pe_m(pe, a, 2)
                if new and k == 6:
                    pe_qkt(pe, j, 2)
                if old and k == 7:
                    pe_ms(pe, a)
                if new:
                    if k == 7:
                        pe_kt(pe, j, 0)
                    if k == 8:
                        pe_st(pe, j, 0)
                        pe_s0(pe, j)
                    if k == 9:
                        pe_s12(pe, j)
                        pe_kt(pe, j, 1)
                    if k == 10:
                        pe_st(pe, j, 1)
                        pe_kt(pe, j, 2)
                    if k == 11:
                        pe_st(pe, j, 2)
                        pe_kt(pe, j, 3)
                        pe_sfin(pe, j, 0)

        AHEAD = {1: (3, 4), 3: (5, 6), 5: (7, 8), 7: (9, 10), 8: (11,), 9: (12,), 10: (13,), 11: (14,)}

        def split_ahead(split, j, k):
            for n in AHEAD.get(k, ()):
                if j + n // 12 < GH:
                    split(("a", j + n // 12, n % 12))

        def act_attention(act, chain, j):
            a, new, old = j - 1, j < GH, j > 0

            def qkt(g):
                w = 3 * j + g
                act.wait_ge(qkt_ready, w + 1)
                if j and g == 0:
                    act.wait_ge(ss_ready, 3 * j)
                act.activation(qkT[:, g, :, 0:TP], X[:, 0:2, :], ACT.Copy)
                act.activation(qkT[:, g, :, TP:T], X[:, 2, 0:2 * TS].rearrange("p (s t) -> p s t", s=2),
                               ACT.Copy).then_inc(qkt_read, 1)

            def pt_out(a, i, s0):
                act.wait_ge(pt_ready, 3 * a + i + 1)
                if i == 2:
                    act.wait_ge(o_ready, 3 * a + 1)
                elif i == 0 and a:
                    act.wait_ge(o_ready, 3 * a)
                act.activation(pt[:, s0:s0 + 2, :], X[:, 0:2, :], ACT.Copy).then_inc(pt_read, 1)

            def kt(n):
                act.wait_ge(kc_t, 4 * j + n + 1)
                if 4 * j + n:
                    act.wait_ge(st_ready, 4 * j + n)
                act.activation(kcT[:].rearrange("p (e b) k -> p e (b k)", e=2), X[:, 0:2, :], ACT.Copy).then_inc(kc_read, 1)

            def st(jj, n):
                act.wait_ge(st_ready, 4 * jj + n + 1)
                if jj:
                    act.wait_ge(ss_ready, 3 * jj)
                act.activation(sts[:, n, :], X[:, 2, n * TS:(n + 1) * TS], ACT.Copy).then_inc(st_read, 1)

            def exps(g):
                act.wait_ge(s_max, 3 * j + g + 1)
                for r in range(CH):
                    x = p0[:, r, :] if g == 0 else p12[:, g - 1, r, :]
                    ins = act.activation(x, x, ACT.Exp, scale=SCALE, bias=nm[:, g, r:r + 1], accum_out=sm[:, g, r:r + 1])
                ins.then_inc(s_exp, 1)

            def exps_s(jj, g):
                act.wait_ge(ss_max, 3 * jj + g + 1)
                x = ps_[0:TS, SEG[g]:SEG[g + 1]]
                act.activation(x, x, ACT.Exp, scale=SCALE, bias=nms[0:TS, g:g + 1],
                               accum_out=sms[0:TS, g:g + 1]).then_inc(ss_exp, 1)

            for k in range(12 if new else 8):
                if new:
                    split_ahead(split_hi, j, k)
                    if k < 6:
                        for c in ((0, 1) if k % 2 == 0 else (2,)):
                            rope_act(act, chain, j, k // 2, c)
                    elif 7 <= k <= 8:
                        if k == 7:
                            if j:
                                act.wait_ge(vc_used, j)
                                act.wait_ge(v_out, 240 * j)
                            act.wait_ge(pj_ready, ticket_a(j, 6) + 1)
                            for g in range(2):
                                ins = act.activation(vr[:, 1 + g, 0:CH, :], PJ[:, 0:2, :].rearrange(
                                    "p e (t g c) -> p g (e t) c", g=2, c=P)[:, g], ACT.Copy)
                            ins.then_inc(pj_read[0], 1)
                            act.wait_ge(pj_ready, ticket_a(j, 7) + 1)
                            act.activation(vr[0:TS, 1:3, CH, :], PJ[0:TS, 2, 0:256].rearrange("p (g c) -> p g c", g=2),
                                           ACT.Copy).then_inc(pj_read[1], 1)
                        else:
                            act.wait_ge(pj_ready, ticket_a(j, 8) + 1)
                            act.activation(vr[:, 0, 0:CH, :], PJ[:, 0, :].rearrange("p (t c) -> p t c", c=P), ACT.Copy)
                            act.activation(vr[0:TS, 0, CH, :], PJ[0:TS, 1, 0:P], ACT.Copy).then_inc(pj_read[0], 1)
                    elif k >= 9:
                        act.wait_ge(pj_ready, ticket_a(j, k) + 1)
                        if 3 * j + k - 9:
                            act.wait_ge(za_done, 3 * j + k - 9)
                        act.activation(halves(zs), pj(k), ACT.Sigmoid).then_inc(za_sig, 1)
                if old:
                    if k == 0:
                        st(a, 3)
                        exps_s(a, 0)
                    if k == 1:
                        exps_s(a, 1)
                        pt_out(a, 0, 0)
                    if k == 2:
                        exps_s(a, 2)
                        pt_out(a, 1, 2)
                        act.wait_ge(cs_in, a + 1)
                        act.activation(wxs[0:TS], wxs[0:TS], ACT.Exp).then_inc(ws_exp, 1)
                if new and k == 3:
                    qkt(0)
                if old and k == 4:
                    pt_out(a, 2, 0)
                    act.wait_ge(pts_ready, a + 1)
                    act.activation(pts[:, 0:4, :], X[:, 2, 0:4 * TS].rearrange("p (n t) -> p n t", n=4), ACT.Copy)
                    act.activation(pts[0:TS, 4:7, :], X[0:TS, 2, 4 * TS:7 * TS].rearrange("p (n t) -> p n t", n=3),
                                   ACT.Copy).then_inc(pts_read, 1)
                if new:
                    if k == 5:
                        qkt(1)
                    if k == 6:
                        qkt(2)
                    if k == 7:
                        kt(0)
                    if k == 8:
                        st(j, 0)
                    if k == 9:
                        exps(0)
                        kt(1)
                    if k == 10:
                        exps(1)
                        exps(2)
                        st(j, 1)
                        kt(2)
                    if k == 11:
                        act.wait_ge(c_in, j + 1)
                        act.activation(wx, wx, ACT.Exp).then_inc(w_exp, 1)
                        st(j, 2)
                        kt(3)

        def dve_attention(dve, chain, j):
            a, new, old = j - 1, j < GH, j > 0

            def mask(g):
                dve.wait_ge(s_ready, 3 * j + g + 1)
                if j:
                    dve.wait_ge(pt_ready, 3 * (j - 1) + (2 if g == 0 else 3))
                    dve.wait_ge(w_exp, j)
                if g == 0:
                    for r in range(CH):
                        d = CH - 1 - r
                        ins = dve.scalar_tensor_tensor(
                            out=p0[:, r, :], in0=m0[:, d:d + CH, :].rearrange("p d k -> p (d k)"), scalar=NEG,
                            in1=X[:, r, :], op0=ALU.mult, op1=ALU.add)
                    x = p0[:]
                else:
                    x = p12[:, g - 1]
                    ins = dve.scalar_tensor_tensor(
                        out=x, in0=m12[:, g - 1, :].unsqueeze(1).to_broadcast([P, CH, P]), scalar=NEG,
                        in1=X[:, 1 + g, :].rearrange("p (r k) -> p r k", k=P), op0=ALU.mult, op1=ALU.add)
                ins.then_inc(s_mask, 1)
                dve.wait_ge(s_mask, 3 * j + g + 1)
                chain(dve.tensor_reduce(out=nm[:, g], in_=x, axis=AX_X, op=ALU.max, negate=True))
                dve.tensor_scalar(nm[:, g], nm[:, g], SCALE, None, ALU.mult).then_inc(s_max, 1)

            def mask_s(jj, g):
                dve.wait_ge(ss_ready, 3 * jj + g + 1)
                if jj:
                    dve.wait_ge(pts_ready, jj)
                    dve.wait_ge(ws_exp, jj)
                c0, c1 = SEG[g], SEG[g + 1]
                x = ps_[0:TS, c0:c1]
                dve.scalar_tensor_tensor(out=x, in0=ms_[:, c0:c1], scalar=NEG, in1=X[0:TS, 3, 0:c1 - c0],
                                         op0=ALU.mult, op1=ALU.add).then_inc(ss_mask, 1)
                dve.wait_ge(ss_mask, 3 * jj + g + 1)
                chain(dve.tensor_reduce(out=nms[0:TS, g:g + 1], in_=x, axis=AX_X, op=ALU.max, negate=True))
                dve.tensor_scalar(nms[0:TS, g:g + 1], nms[0:TS, g:g + 1], SCALE, None, ALU.mult).then_inc(ss_max, 1)

            def weigh(n, nmx, w, low, n_max, maxes, done):
                dve.wait_ge(n_max, maxes)
                chain(dve.tensor_tensor(low, nmx[:, 0], nmx[:, 1], ALU.min))
                chain(dve.tensor_tensor(low, low, nmx[:, 2], ALU.min))
                dve.tensor_tensor(w, low.unsqueeze(1).to_broadcast([n, 3, low.shape[1]]), nmx, ALU.subtract).then_inc(done, 1)

            def factors(n, w, s, c, d):
                chain(dve.tensor_tensor(c, w, s, ALU.mult))
                chain(dve.tensor_tensor(d, c[:, 0], c[:, 1], ALU.add))
                chain(dve.tensor_tensor(d, d, c[:, 2], ALU.add))
                chain(dve.reciprocal(d, d))
                chain(dve.tensor_tensor(c, w, d.unsqueeze(1).to_broadcast([n, 3, d.shape[1]]), ALU.mult))

            def gate_o(g):
                dve.wait_ge(o_ready, 3 * a + g + 1)
                z = oz[:, g * GH + a, 0:TP]
                dve.tensor_tensor(z, z, X[:, 3, :], ALU.mult).then_inc(o_read, 1)

            for k in range(12 if new else 8):
                if new:
                    split_ahead(split_lo, j, k)
                    if k < 6:
                        for c in ((0, 1) if k % 2 == 0 else (2,)):
                            rope_dve(dve, chain, j, k // 2, c)
                    elif k >= 9:
                        dve.wait_ge(za_sig, 3 * j + k - 8)
                        dve.tensor_tensor(halves(zs), pj(k), halves(zs), ALU.mult).then_inc(pj_read[k % 2], 1)
                        wait_read(dve, ticket_a(j, k))
                        dve.tensor_copy(oz[:, (k - 9) * GH + j, :], zs).then_inc(za_done, 1)
                if old:
                    if k == 0:
                        mask_s(a, 1)
                    if k == 1:
                        mask_s(a, 2)
                        v = lambda x: x[0:TS].unsqueeze(2)
                        weigh(TS, v(nms), v(wxs), mns[0:TS], ss_max, 3 * a + 3, cs_in)
                    if k == 3:
                        gate_o(0)
                        dve.wait_ge(ws_exp, a + 1)
                        dve.wait_ge(ss_exp, 3 * a + 3)
                        factors(TS, v(wxs), v(sms), v(cxs), dens[0:TS])
                        for g in range(3):
                            x = ps_[0:TS, SEG[g]:SEG[g + 1]]
                            ins = dve.tensor_scalar(x, x, cxs[0:TS, g:g + 1], None, ALU.mult)
                        ins.then_inc(ps_scaled, 1)
                    if k == 5:
                        gate_o(1)
                    if k == 6:
                        gate_o(2)
                    if k == 7:
                        dve.wait_ge(vc_used, a + 1)
                        z = oz[:, a:BH:GH, TP:T]
                        dve.tensor_tensor(z, z, X[:, 3, 0:3 * TS].rearrange("p (g t) -> p g t", g=3),
                                          ALU.mult).then_inc(os1_read, 1)
                if new:
                    if k == 8:
                        mask(0)
                    if k == 9:
                        mask(1)
                        mask(2)
                        weigh(P, nm, wx, mn, s_max, 3 * j + 3, c_in)
                    if k == 11:
                        dve.wait_ge(w_exp, j + 1)
                        dve.wait_ge(s_exp, 3 * j + 3)
                        factors(P, wx, sm, cx, den)
                        dve.tensor_tensor(p0[:], p0[:], cx[:, 0].unsqueeze(2).to_broadcast([P, CH, TP]),
                                          ALU.mult).then_inc(p_scaled, 1)
                        dve.tensor_tensor(p12[:], p12[:], cx[:, 1:3].unsqueeze(3).to_broadcast([P, 2, CH, P]),
                                          ALU.mult).then_inc(p_scaled, 1)
                        mask_s(j, 0)

        def attention_tables(dve, chain):
            dve.wait_ge(a_const, 16 * 7)
            h = BHD // 2
            cos, sin = cs_raw[:, 0], cs_raw[:, 1]
            for s in range(2):
                for x in range(2):
                    w, w2 = (qkw[:, s, y * h:(y + 1) * h].unsqueeze(1).to_broadcast([P, CH + 1, h]) for y in (x, 1 - x))
                    dve.tensor_tensor(tcos[:, :, s, x * h:(x + 1) * h], cos, w, ALU.mult)
                    last = dve.scalar_tensor_tensor(out=tsin[:, :, s, x * h:(x + 1) * h], in0=sin,
                                                    scalar=-1.0 if x == 0 else 1.0, in1=w2, op0=ALU.mult, op1=ALU.mult)
            for mask, there, _ in masks:
                last = dve.tensor_copy(mask, there)
            last.then_inc(tab_done, 1)

        def load_attention_constants(sp):
            sp.wait_ge(n_lo, 2 * KD)
            sp.wait_ge(n_hx, 2 * KD)
            sp.wait_ge(parked1, 16)
            for dst, src in ((cs_raw[:, 0], I["c_cos"]), (cs_raw[:, 1], I["c_sin"]),
                             *((there, src) for _, there, src in masks),
                             (qkw[:, 0], I["b_q_norm_w"].partition_broadcast(P)),
                             (qkw[:, 1], I["b_k_norm_w"].partition_broadcast(P))):
                sp.dma_start(dst, src).then_inc(a_const, 16)

        def pe_y(pe, m):
            wait_read(pe, OUT1 + m)
            if m >= 2:
                pe.wait_ge(y_read, m - 1)
            bank = 2 * (m % 2)
            for t in range(CH):
                pe.transpose(X[:, bank, t * P:(t + 1) * P], xT2[:, m, t * P:(t + 1) * P], ident[:])
            pe.transpose(X[0:TS, bank + 1, 0:P], xT2[:, m, TP:T], ident[:]).then_inc(y_t, 1)

        def act_y(act, m):
            act.wait_ge(y_t, m + 1)
            bank = 2 * (m % 2)
            if m >= 2:
                act.wait_ge(y_out[m % 2], 32 * (m // 2))
            act.activation(yr[:, m % 2, 0:CH, :], X[:, bank, :].rearrange("p (t f) -> p t f", t=CH), ACT.Copy)
            act.activation(yr[0:TS, m % 2, CH, :], X[0:TS, bank + 1, 0:P], ACT.Copy).then_inc(y_read, 1)

        def store_y(act, m):
            act.wait_ge(y_read, m + 1)
            f = slice(m * P, (m + 1) * P)
            act.dma_start(O["y_prompt"][0, :, f].rearrange("(t p) f -> p t f", p=P),
                         yr[:, m % 2, 0:CH, :]).then_inc(y_out[m % 2], 16)
            act.dma_start(O["y_sample"][:, :, f].rearrange("b t f -> (b t) f"),
                         yr[0:TS, m % 2, CH, :]).then_inc(y_out[m % 2], 16)

        block = ctx.enter_context(nc.Block())

        @block.sync
        def _(sp):
            sp.dma_start(c_row[0:1, :], I["c_prompt"]).then_inc(s_c, 16)
            sp.dma_start(c_row[1:NC_, :], I["c_sample"]).then_inc(s_c, 16)
            sp.dma_start(ident[:], I["c_ident"]).then_inc(s_c, 16)
            sp.dma_start(adab[:], I["ada_b"].rearrange("l (m p) -> p l m", p=P)).then_inc(s_const, 16)
            sp.dma_start(normw[:], I["norm_w"].rearrange("l (m p) -> p l m", p=P)).then_inc(s_const, 16)
            for n, (key, src, nk, width, freed) in enumerate(stream):
                if n == 3:
                    sp.dma_start(x_row[:, 0:4, :], I["x_prompt"][0].rearrange("(t p) f -> p t f", p=P)).then_inc(s_x, 16)
                    sp.dma_start(x_row[0:TS, 4, :], I["x_sample"].rearrange("b t f -> (b t) f")).then_inc(s_x, 16)
                if n >= RAWS:
                    s, value = stream[n - RAWS][4]
                    sp.wait_ge(s, value)
                dst = raw_of(key)
                if loads_of(src) == 2:
                    for x in range(2):
                        sp.dma_start(dst[:, :, x * P:(x + 1) * P], src[:, :, x, :]).then_inc(raw_in[n % RAWS], 16)
                else:
                    sp.dma_start(dst, src).then_inc(raw_in[n % RAWS], 16)
                if key == ("w", 0, 0):
                    sp.wait_ge(x_sb, KD)
                    sp.dma_start(xpark, xT[:].rearrange("p k t -> p (k t)")).then_inc(parked, 16)
                if key == ("w", 0, 2):
                    sp.wait_ge(n_lo, KD)
                    sp.wait_ge(parked, 16)
                    sp.dma_start(lev_raw, I["c_levels"]).then_inc(s_const, 16)
                    sp.dma_start(reset[:], I["c_reset"].partition_broadcast(P)).then_inc(s_const, 16)
                    sp.dma_start(seqm[:], I["c_seq"]).then_inc(s_const, 16)
                    sp.dma_start(lbr[:], I["a_lower_bounds"].rearrange("l (h p) -> p l h", p=P)).then_inc(s_const, 16)
                    sp.dma_start(bf[:], I["a_b_f"][0].rearrange("(h p) -> p h", p=P)).then_inc(s_const, 16)
                    sp.dma_start(gw[:], I["a_g_norm_w"][0].rearrange("(j p) -> p j", p=P)).then_inc(s_const, 16)
                if key == ("out0", 0, 1):
                    sp.wait_ge(fin_done, 2 * AH)
                    sp.wait_ge(sp_out, 16 * AH)
                    sp.wait_ge(s0_out[0], 16 * AH // 2)
                    sp.wait_ge(s0_out[1], 16 * AH // 2)
                    sp.dma_start(xT1[:].rearrange("p k t -> p (k t)"), xpark).then_inc(unparked, 16)
                if key[0] == "w" and key[2] == 5:
                    h = key[1]
                    if h >= 2:
                        sp.wait_ge(s0_out[h % 2], 16 * (h // 2))
                    sp.dma_start(s0[:, h % 2], I["state_hgrn"][0, :, h].rearrange("b k v -> k b v")).then_inc(s0_in[h % 2], 16)
                if key == ("a", 0, 0):
                    wait_read(sp, OUT0 + 6)
                    wait_read(sp, OUT0 + 7)
                    sp.dma_start(xpark1, xT1[:].rearrange("p k t -> p (k t)")).then_inc(parked1, 16)
                if key == ("a", 0, 2):
                    load_attention_constants(sp)
                for what, args in after.get(n, ()):
                    what(sp, *args)
                if key == ("out1", 1, 0):
                    sp.wait_ge(os1_read, GH)
                    sp.wait_ge(k_out[0], 80 * 6)
                    sp.wait_ge(k_out[1], 80 * 6)
                    sp.wait_ge(v_out, 240 * GH)
                    sp.dma_start(xT2[:].rearrange("p k t -> p (k t)"), xpark1).then_inc(unparked1, 16)
            for x in range(2):
                sp.wait_ge(y_out[x], 32 * (KD // 2))

        @block.gpsimd
        def _(pool):
            nc.gpsimd.memset(ones[:], 1.0).then_inc(ones_done, 1)
            nc.gpsimd.memset(eps[:], EPS).then_inc(ones_done, 1)
            nc.gpsimd.memset(h_hi[:, :, T:TPAD].bitcast(F32), 0.0).then_inc(ones_done, 1)
            nc.gpsimd.memset(h_lo[:, :, T:TPAD].bitcast(F32), 0.0).then_inc(ones_done, 1)
            for h in range(AH):
                pool_scan(pool, h)
            pool.wait_ge(tab_done, 1)
            for j in range(GH):
                for g in range(3):
                    for c in range(3):
                        rope_pool(pool, j, g, c)

        @block.scalar
        def _(act):
            chain = Count(act, act_ch)
            act.wait_ge(s_c, 48)
            act.activation(c_sg[:], c_row[:], ACT.Sigmoid).then_inc(c_sig, 1)
            for k in range(KD):
                act.wait_ge(x_t, k + 1)
                chain(act.activation(xT[:, k, 0:TP], PJ[:, 2 * (k % 2), :], ACT.Copy))
                act.activation(xT[:, k, TP:T], PJ[:, 2 * (k % 2) + 1, 0:TS], ACT.Copy).then_inc(x_sb, 1)
            act.wait_ge(ones_done, 2)
            norm_act(0, xT, nsq, rn, xr, hf, chain, lambda e, k: e.wait_ge(x_sb, k + 1))
            for p in range(3):
                split_hi(("w", 0, p))
            act.wait_ge(lb_in, 1)
            act.activation(lb[:], lb[:], ACT.Exp).then_inc(lb_exp, 1)
            for h in range(AH + 2):
                act_step(act, chain, h)
            norm_act(1, xT1, nsq1, rn1, xr1, hf1, chain, lambda e, k: wait_read(e, OUT0 + k))
            for p in range(3):
                split_hi(("a", 0, p))
            act.wait_ge(tab_done, 1)
            for j in range(GH + 1):
                act_attention(act, chain, j)
            for m in range(KD):
                act_y(act, m)
                store_y(act, m)

        @block.vector
        def _(dve):
            chain = Count(dve, dve_ch)
            dve.wait_ge(c_sig, 1)
            dve.tensor_tensor(c_sg[:], c_sg[:], c_row[:], ALU.mult).then_inc(c_silu, 1)
            dve.wait_ge(c_t, 1)
            dve.tensor_copy(scT[:], X[:, 3, 0:KD * NC_].rearrange("p (k n) -> p k n", k=KD)).then_inc(c_sb, 1)
            dve.wait_ge(s_const, 32)
            dve.wait_ge(raw_used, 16)
            read_ada(0, 0, 16)
            dve.wait_ge(ada_done, 1)
            make_amp(0, chain)
            dve.wait_ge(amp_done, 1)
            norm_dve(0, xT, rn, xr, hf, chain)
            for p in range(3):
                split_lo(("w", 0, p))
            dve.wait_ge(s_const, 16 * 8)
            chain(dve.tensor_copy(lev[:].rearrange("p l t -> p (l t)"), lev_raw))
            chain(dve.tensor_tensor(lb[:, 0], lbr[:, 0], lbr[:, 1], ALU.max))
            chain(dve.tensor_tensor(lbr[:], lbr[:], lb[:, 0].unsqueeze(1).to_broadcast([P, 2, AH]), ALU.subtract))
            dve.tensor_copy(lb[:], lbr[:]).then_inc(lb_in, 1)
            dve.wait_ge(lb_exp, 1)
            chain(dve.tensor_tensor(lbr[:, 0], lb[:, 0], lb[:, 1], ALU.add))
            chain(dve.reciprocal(lbr[:, 1], lbr[:, 0]))
            chain(dve.tensor_tensor(lb[:, 0], lb[:, 0], lbr[:, 1], ALU.mult))
            chain(dve.tensor_scalar(lb[:, 1], lb[:, 0], -1.0, 1.0, ALU.mult, ALU.add))
            for h in range(AH + 2):
                dve_step(dve, chain, h)
            for m in range(KD):
                if m == 0:
                    dve.wait_ge(unparked, 16)
                dve_residual(dve, chain, 0, OUT0 + m, m, xT1, yg)
            make_amp(1, chain)
            dve.wait_ge(amp_done, 2)
            norm_dve(1, xT1, rn1, xr1, hf1, chain)
            for p in range(3):
                split_lo(("a", 0, p))
            attention_tables(dve, chain)
            dve.wait_ge(tab_done, 1)
            for j in range(GH + 1):
                dve_attention(dve, chain, j)
            dve.wait_ge(unparked1, 16)
            for m in range(KD):
                dve_residual(dve, chain, 1, OUT1 + m, m, xT2, yg2)

        @block.tensor
        def _(pe):
            pe.wait_ge(c_silu, 1)
            pe.wait_ge(s_c, 48)
            for k in range(KD):
                last = pe.transpose(X[:, 3, k * NC_:(k + 1) * NC_], c_sg[:, k * P:(k + 1) * P], ident[0:NC_, 0:NC_])
            last.then_inc(c_t, 1)
            pe.wait_ge(s_x, 32)
            for k in range(KD):
                if k >= 2:
                    pe.wait_ge(x_sb, k - 1)
                for t in range(CH):
                    pe.transpose(PJ[:, 2 * (k % 2), t * P:(t + 1) * P], x_row[:, t, k * P:(k + 1) * P], ident[:])
                pe.transpose(PJ[:, 2 * (k % 2) + 1, 0:TS], x_row[0:TS, CH, k * P:(k + 1) * P],
                             ident[0:TS, 0:TS]).then_inc(x_t, 1)
            pe.wait_ge(c_sb, 1)
            pe.wait_ge(x_sb, KD)
            for n in range(16):
                project_ada(n)
            pe.wait_ge(ones_done, 4)
            norm_pe(0, nsq)
            pe.wait_ge(n_lo, KD)
            pe.wait_ge(n_hx, KD)
            for h in range(AH + 2):
                pe_step(pe, h)
            pe.wait_ge(fin_done, 2 * AH)
            pe_out(pe, "out0", OUT0, 8)
            norm_pe(1, nsq1)
            pe.wait_ge(n_lo, 2 * KD)
            pe.wait_ge(n_hx, 2 * KD)
            for j in range(GH + 1):
                pe_attention(pe, j)
            pe.wait_ge(os1_read, GH)
            pe_out(pe, "out1", OUT1, 6, then=lambda m: m and pe_y(pe, m - 1))
            pe_y(pe, KD - 1)


INPUTS = ("x_prompt", "x_sample", "state_hgrn", "cache_kv_w128", "cache_kv_w512", "cache_kv_w2048", "c_prompt",
          "c_sample", "norm_w", "ada_w", "ada_b", "a_lower_bounds", "a_w_in", "a_b_f", "a_g_norm_w", "a_w_out",
          "b_w_in", "b_q_norm_w", "b_k_norm_w", "b_w_out")
OUTPUTS = (("y_prompt", (1, TP, D)), ("y_sample", (DB, DS, D)),
           ("hgrn_prompt", (1, 1, AH, ADK, ADV)), ("hgrn_sample", (1, DB, AH, ADK, ADV)),
           ("kv128_prompt", (1, 1, 128, 2, GH, BHD)), ("kv128_sample", (1, DB, DS, 2, GH, BHD)),
           ("kv512_prompt", (1, 1, TP, 2, GH, BHD)), ("kv512_sample", (1, DB, DS, 2, GH, BHD)),
           ("kv2048_prompt", (1, 1, TP, 2, GH, BHD)), ("kv2048_sample", (1, DB, DS, 2, GH, BHD)))


def kernel(**inputs):
    import concourse.bacc as bacc
    from concourse.bass_utils import run_bass_kernel_spmd

    nc = bacc.Bacc("TRN2", target_bir_lowering=False, num_devices=1)
    arrays, I, O = {}, {}, {}
    given = {name: np.ascontiguousarray(inputs[name]) for name in INPUTS}
    given.update(constants())
    for name, a in given.items():
        arrays[f"in_{name}_dram"] = a
        I[name] = nc.dram_tensor(f"in_{name}_dram", a.shape, mybir.dt.from_np(a.dtype), kind="ExternalInput").ap()
    for name, shape in OUTPUTS:
        O[name] = nc.dram_tensor(f"out_{name}_dram", shape, F32, kind="ExternalOutput").ap()
    program(nc, I, O)
    got = run_bass_kernel_spmd(nc, [arrays], core_ids=[0]).results[0]
    return tuple(got[f"out_{name}_dram"] for name, _ in OUTPUTS)
```
